# Optimizing a Trainium2 kernel written in Bass

```python
import math
import jax, jax.numpy as jnp
from jax import lax
import numpy as np

D_MODEL = 2048
BATCH = 1
SEQ = 256
DEPTH = 1

HG_HEADS = 16
HG_KDIM = 128
HG_VDIM = 128
HG_WIDTH = HG_HEADS * HG_KDIM
HG_CHUNK = 64
ATTN_GROUPS = ((128, 1), (512, 4), (2048, 16))
ATTN_HEADS_PER_GROUP = 4
HEAD_DIM = 128
ATTN_WIDTH = len(ATTN_GROUPS) * ATTN_HEADS_PER_GROUP * HEAD_DIM
ATTN_OUT = ATTN_HEADS_PER_GROUP * HEAD_DIM
ROPE_THETA = 10000.0
D_FF = 5632
CONV_WIDTH = 3
NORM_EPS = 1e-6
NEG_INF = -1e30
IN_COLS = 4 * HG_WIDTH + 3 * ATTN_WIDTH + 2 * D_MODEL


def rmsnorm(x, g):
    x32 = x.astype(jnp.float32)
    y = x32 * lax.rsqrt(jnp.mean(x32 * x32, axis=-1, keepdims=True) + NORM_EPS)
    return (y * g.astype(jnp.float32)).astype(x.dtype)

def rope(x):
    T, Dh = x.shape[1], x.shape[-1]
    half = Dh // 2
    inv_freq = jnp.exp(-math.log(ROPE_THETA) * jnp.arange(half, dtype=jnp.float32) * (2.0 / Dh))
    ang = jnp.arange(T, dtype=jnp.float32)[:, None] * inv_freq[None, :]
    cos = jnp.cos(ang)[None, :, None, :]
    sin = jnp.sin(ang)[None, :, None, :]
    x32 = x.astype(jnp.float32)
    x1, x2 = x32[..., :half], x32[..., half:]
    return jnp.concatenate([x1 * cos - x2 * sin, x2 * cos + x1 * sin], axis=-1).astype(x.dtype)

def hgrn2_branch(q_raw, f_raw, i_raw, g_raw, lb, norm_g):
    B, T, _ = q_raw.shape
    H, K, V, C = HG_HEADS, HG_KDIM, HG_VDIM, HG_CHUNK
    N = T // C
    f32 = jnp.float32
    z = f_raw.astype(f32)
    lb = lb.astype(f32)
    log_f = jnp.logaddexp(jnp.log(lb), jnp.log1p(-lb) + jax.nn.log_sigmoid(z))
    k = (1.0 - lb) * jax.nn.sigmoid(-z)
    q = jax.nn.silu(q_raw.astype(f32))
    v = i_raw.astype(f32)

    def chunks(a, dim):
        return a.reshape(B, N, C, H, dim).transpose(1, 0, 3, 2, 4)

    xs = (chunks(q, K), chunks(k, K), chunks(log_f, K), chunks(v, V))
    causal = jnp.tril(jnp.ones((C, C), dtype=bool))[:, :, None]

    def step(S, inp):
        qc, kc, gc, vc = inp
        G = jnp.cumsum(gc, axis=-2)
        G_last = G[..., -1:, :]
        rel = G[..., :, None, :] - G[..., None, :, :]
        decay = jnp.exp(jnp.where(causal, rel, NEG_INF))
        A = jnp.einsum('bhtk,bhsk,bhtsk->bhts', qc, kc, decay)
        o = (jnp.einsum('bhts,bhsv->bhtv', A, vc)
             + jnp.einsum('bhtk,bhkv->bhtv', qc * jnp.exp(G), S))
        S = (jnp.exp(G_last)[..., 0, :, None] * S
             + jnp.einsum('bhsk,bhsv->bhkv', kc * jnp.exp(G_last - G), vc))
        return S, o

    S0 = jnp.zeros((B, H, K, V), f32)
    _, o = lax.scan(step, S0, xs)
    o = o.transpose(1, 0, 3, 2, 4).reshape(B, T, H, V)
    o = o * lax.rsqrt(jnp.mean(o * o, axis=-1, keepdims=True) + NORM_EPS) * norm_g.astype(f32)
    o = o * jax.nn.silu(g_raw.astype(f32).reshape(B, T, H, V))
    return o.reshape(B, T, H * V).astype(q_raw.dtype)

def banded_causal_attention(q, k, v, steps):
    P = steps
    L, Dh = q.shape[-2], q.shape[-1]
    lead = q.shape[:-2]
    n = -(-L // P)
    Lp = n * P
    nd = len(lead)
    qp = jnp.pad(q, [(0, 0)] * nd + [(0, Lp - L), (0, 0)])
    kp = jnp.pad(k, [(0, 0)] * nd + [(P, Lp - L), (0, 0)])
    vp = jnp.pad(v, [(0, 0)] * nd + [(P, Lp - L), (0, 0)])
    qb = qp.reshape(lead + (n, P, Dh))

    def band(a):
        return jnp.concatenate([a[..., :Lp, :].reshape(lead + (n, P, Dh)),
                                a[..., P:, :].reshape(lead + (n, P, Dh))], axis=-2)

    kb, vb = band(kp), band(vp)
    s = jnp.einsum('...nqd,...nkd->...nqk', qb, kb).astype(jnp.float32) * (Dh ** -0.5)
    q_pos = jnp.arange(n)[:, None] * P + jnp.arange(P)[None, :]
    k_pos = jnp.arange(n)[:, None] * P - P + jnp.arange(2 * P)[None, :]
    rel = q_pos[:, :, None] - k_pos[:, None, :]
    mask = (rel >= 0) & (rel <= steps) & (k_pos[:, None, :] >= 0)
    s = jnp.where(mask, s, NEG_INF)
    lse = jax.nn.logsumexp(s, axis=-1)
    p = jnp.exp(s - lse[..., None])
    o = jnp.einsum('...nqk,...nkd->...nqd', p, vb.astype(jnp.float32))
    o = o.reshape(lead + (Lp, Dh))[..., :L, :]
    lse = lse.reshape(lead + (Lp,))[..., :L]
    return o, lse

def dilated_attention_branch(q_raw, k_raw, v_raw):
    B, T, _ = q_raw.shape
    G, Hg, Dh = len(ATTN_GROUPS), ATTN_HEADS_PER_GROUP, HEAD_DIM
    q = rope(q_raw.reshape(B, T, G * Hg, Dh)).reshape(B, T, G, Hg, Dh)
    k = rope(k_raw.reshape(B, T, G * Hg, Dh)).reshape(B, T, G, Hg, Dh)
    v = v_raw.reshape(B, T, G, Hg, Dh)
    outs, lses = [], []
    for g, (window, dil) in enumerate(ATTN_GROUPS):
        L = T // dil

        def strided(a):
            return a.reshape(B, L, dil, Hg, Dh).transpose(0, 2, 3, 1, 4)

        o, lse = banded_causal_attention(strided(q[:, :, g]), strided(k[:, :, g]),
                                         strided(v[:, :, g]), window // dil)
        outs.append(o.transpose(0, 3, 1, 2, 4).reshape(B, T, Hg, Dh))
        lses.append(lse.transpose(0, 3, 1, 2).reshape(B, T, Hg))
    alpha = jax.nn.softmax(jnp.stack(lses, axis=0), axis=0)
    o = jnp.sum(alpha[..., None] * jnp.stack(outs, axis=0), axis=0)
    return o.reshape(B, T, Hg * Dh).astype(q_raw.dtype)

def conv_ffn(u, w_up, conv_w, conv_b, w_down):
    hup = u @ w_up
    C = hup.shape[-1]
    hc = lax.conv_general_dilated(hup, conv_w[:, None, :], window_strides=(1,),
                                  padding=[(CONV_WIDTH - 1, 0)],
                                  dimension_numbers=('NWC', 'WIO', 'NWC'),
                                  feature_group_count=C) + conv_b
    a, b = hc[..., :D_FF], hc[..., D_FF:]
    return (jax.nn.gelu(a) * b) @ w_down

def first_inputs(seed: int = 0) -> dict:
    key = jax.random.key(seed)
    ks = jax.random.split(key, 14)
    nrm = jax.random.normal
    f32 = jnp.float32
    return {
        'x': nrm(ks[0], (BATCH, SEQ, D_MODEL), f32),
        'norm1_g': 1.0 + 0.02 * nrm(ks[1], (DEPTH, D_MODEL), f32),
        'w_in': nrm(ks[2], (DEPTH, D_MODEL, IN_COLS), f32) * D_MODEL ** -0.5,
        'hg_lb_param': 0.5 * nrm(ks[3], (DEPTH + 1, HG_WIDTH), f32),
        'hg_norm_g': 1.0 + 0.02 * nrm(ks[4], (DEPTH, HG_VDIM), f32),
        'w_proj_a': nrm(ks[5], (DEPTH, HG_WIDTH, D_MODEL), f32) * HG_WIDTH ** -0.5,
        'w_proj_b': nrm(ks[6], (DEPTH, ATTN_OUT, D_MODEL), f32) * ATTN_OUT ** -0.5,
        'w_out': nrm(ks[7], (DEPTH, D_MODEL, D_MODEL), f32) * D_MODEL ** -0.5,
        'norm2_g': 1.0 + 0.02 * nrm(ks[8], (DEPTH, D_MODEL), f32),
        'w_up': nrm(ks[9], (DEPTH, D_MODEL, 2 * D_FF), f32) * D_MODEL ** -0.5,
        'conv_w': nrm(ks[10], (DEPTH, CONV_WIDTH, 2 * D_FF), f32) * CONV_WIDTH ** -0.5,
        'conv_b': 0.01 * nrm(ks[11], (DEPTH, 2 * D_FF), f32),
        'w_down': nrm(ks[12], (DEPTH, D_FF, D_MODEL), f32) * D_FF ** -0.5,
        'norm_f_g': 1.0 + 0.02 * nrm(ks[13], (D_MODEL,), f32),
    }

def first_block(x, norm1_g, w_in, hg_lb_param, hg_norm_g, w_proj_a, w_proj_b, w_out,
              norm2_g, w_up, conv_w, conv_b, w_down, norm_f_g):
    lower_bounds = jnp.cumsum(jax.nn.softmax(hg_lb_param.astype(jnp.float32), axis=0), axis=0)
    sizes = (HG_WIDTH,) * 4 + (ATTN_WIDTH,) * 3 + (D_MODEL,) * 2
    offsets = [int(o) for o in np.cumsum(sizes)[:-1]]
    h = x
    for l in range(DEPTH):
        u = rmsnorm(h, norm1_g[l])
        proj = u @ w_in[l]
        hq, hf, hi, hg, aq, ak, av, gate_a, gate_b = jnp.split(proj, offsets, axis=-1)
        ya = hgrn2_branch(hq, hf, hi, hg, lower_bounds[l], hg_norm_g[l]) @ w_proj_a[l]
        yb = dilated_attention_branch(aq, ak, av) @ w_proj_b[l]
        mix = jax.nn.sigmoid(gate_a) * ya + jax.nn.sigmoid(gate_b) * yb
        h = h + (mix @ w_out[l]).astype(h.dtype)
        v = rmsnorm(h, norm2_g[l])
        h = h + conv_ffn(v, w_up[l], conv_w[l], conv_b[l], w_down[l]).astype(h.dtype)
    return rmsnorm(h, norm_f_g)


MIX_WIDTH = D_MODEL
LRU_WIDTH = MIX_WIDTH // 2
GMLP_WIDTH = MIX_WIDTH - LRU_WIDTH
IN_WIDTH = 2 * LRU_WIDTH + 2 * GMLP_WIDTH
LRU_HEADS = 8
LRU_HEAD_DIM = LRU_WIDTH // LRU_HEADS
CONV_WIDTH_2 = 4
CONV_LEFT = 2
LRU_C = 8.0
GMLP_HEADS = 8
GMLP_HEAD_DIM = GMLP_WIDTH // GMLP_HEADS
CHUNK = 128
PEER_HEADS = 8
PEER_KEYS = 128
PEER_EXPERTS = PEER_KEYS * PEER_KEYS
PEER_TOPK = 16
PEER_QDIM = 256
PEER_HALF = PEER_QDIM // 2
PEER_BLOCK = 128
EPS = 1e-6


def rms_norm(x, g):
    xf = x.astype(jnp.float32)
    y = xf * lax.rsqrt(jnp.mean(xf * xf, axis=-1, keepdims=True) + EPS)
    return (y * g.astype(jnp.float32)).astype(x.dtype)

def layer_norm(x, g, b):
    xf = x.astype(jnp.float32)
    mu = jnp.mean(xf, axis=-1, keepdims=True)
    xc = xf - mu
    y = xc * lax.rsqrt(jnp.mean(xc * xc, axis=-1, keepdims=True) + EPS)
    return (y * g.astype(jnp.float32) + b.astype(jnp.float32)).astype(x.dtype)

def centred_depthwise_conv(x, w, b):
    S = x.shape[1]
    xp = jnp.pad(x, ((0, 0), (CONV_LEFT, CONV_WIDTH_2 - 1 - CONV_LEFT), (0, 0)))
    y = b + xp[:, 0:S] * w[0]
    for k in range(1, CONV_WIDTH_2):
        y = y + xp[:, k:k + S] * w[k]
    return y

def _recurrence_combine(left, right):
    a_l, b_l = left
    a_r, b_r = right
    return a_l * a_r, a_r * b_l + b_r

def rglru(x, w_a, b_a, w_x, b_x, lam, reverse):
    B, S, _ = x.shape
    xh = x.reshape(B, S, LRU_HEADS, LRU_HEAD_DIM)
    r = jax.nn.sigmoid(jnp.einsum('bshc,hce->bshe', xh, w_a.astype(jnp.float32)).reshape(B, S, LRU_WIDTH) + b_a.astype(jnp.float32))
    i = jax.nn.sigmoid(jnp.einsum('bshc,hce->bshe', xh, w_x.astype(jnp.float32)).reshape(B, S, LRU_WIDTH) + b_x.astype(jnp.float32))
    log_a = -LRU_C * jax.nn.softplus(-lam.astype(jnp.float32)) * r
    a = jnp.exp(log_a)
    u = jnp.sqrt(-jnp.expm1(2.0 * log_a)) * (i * x)
    _, h = lax.associative_scan(_recurrence_combine, (a, u), reverse=reverse, axis=1)
    return h

def recurrent_group(xr, gr, conv_w, conv_b, w_a, b_a, w_x, b_x, lam):
    xc = centred_depthwise_conv(xr, conv_w, conv_b).astype(jnp.float32)
    h = (rglru(xc, w_a[0], b_a[0], w_x[0], b_x[0], lam[0], reverse=False)
         + rglru(xc, w_a[1], b_a[1], w_x[1], b_x[1], lam[1], reverse=True))
    return (jax.nn.gelu(gr.astype(jnp.float32)) * h).astype(xr.dtype)

def spatial_gating_group(gu, gv, ln_g, ln_b, w_s, b_s):
    B, S, _ = gv.shape
    u = jax.nn.gelu(gu)
    v = layer_norm(jax.nn.gelu(gv), ln_g, ln_b)
    vc = v.reshape(B, S // CHUNK, CHUNK, GMLP_HEADS, GMLP_HEAD_DIM)
    mixed = jnp.einsum('hpq,bnqhc->bnphc', w_s, vc) + b_s.T[None, None, :, :, None]
    return u * mixed.reshape(B, S, GMLP_WIDTH)

def peer(x, w_q, sub_keys, expert_u, expert_v):
    B, S, D = x.shape
    q = (x @ w_q).reshape(B, S, PEER_HEADS, 2, PEER_HALF)
    s = jnp.einsum('bshpk,hpnk->bshpn', q, sub_keys).astype(jnp.float32)
    top_s, top_i = lax.top_k(s, PEER_TOPK)
    cand_s = (top_s[..., 0, :, None] + top_s[..., 1, None, :]).reshape(B, S, PEER_HEADS, PEER_TOPK * PEER_TOPK)
    cand_i = (top_i[..., 0, :, None] * PEER_KEYS + top_i[..., 1, None, :]).reshape(B, S, PEER_HEADS, PEER_TOPK * PEER_TOPK)
    best_s, pos = lax.top_k(cand_s, PEER_TOPK)
    ids = jnp.take_along_axis(cand_i, pos, axis=-1)
    g = jax.nn.softmax(best_s, axis=-1).astype(x.dtype)
    n_blk = (B * S) // PEER_BLOCK
    xb = x.reshape(n_blk, PEER_BLOCK, D)
    ib = ids.reshape(n_blk, PEER_BLOCK, PEER_HEADS * PEER_TOPK)
    gb = g.reshape(n_blk, PEER_BLOCK, PEER_HEADS * PEER_TOPK)

    def block(args):
        xt, it, gt = args
        u = jnp.take(expert_u, it, axis=0)
        act = jax.nn.gelu(jnp.einsum('td,tkd->tk', xt, u)) * gt
        v = jnp.take(expert_v, it, axis=0)
        return jnp.einsum('tk,tkd->td', act, v)

    out = lax.map(block, (xb, ib, gb))
    return out.reshape(B, S, D)

def second_inputs(seed: int = 0) -> dict:
    key = jax.random.key(seed)
    ks = jax.random.split(key, 24)
    f32 = jnp.float32
    nrm = lambda k, shape, scale: jax.random.normal(k, shape, f32) * scale
    lam_u = jax.random.uniform(ks[10], (DEPTH, 2, LRU_WIDTH), f32, minval=0.9, maxval=0.999)
    lam_base = lam_u ** (1.0 / LRU_C)
    return {
        "x": nrm(ks[0], (BATCH, SEQ, D_MODEL), 1.0),
        "mix_norm_g": 1.0 + nrm(ks[1], (DEPTH, D_MODEL), 0.02),
        "w_in": nrm(ks[2], (DEPTH, D_MODEL, IN_WIDTH), D_MODEL ** -0.5),
        "conv_w": nrm(ks[3], (DEPTH, CONV_WIDTH_2, LRU_WIDTH), CONV_WIDTH_2 ** -0.5),
        "conv_b": nrm(ks[4], (DEPTH, LRU_WIDTH), 0.02),
        "lru_w_a": nrm(ks[5], (DEPTH, 2, LRU_HEADS, LRU_HEAD_DIM, LRU_HEAD_DIM), LRU_HEAD_DIM ** -0.5),
        "lru_b_a": nrm(ks[6], (DEPTH, 2, LRU_WIDTH), 0.02),
        "lru_w_x": nrm(ks[7], (DEPTH, 2, LRU_HEADS, LRU_HEAD_DIM, LRU_HEAD_DIM), LRU_HEAD_DIM ** -0.5),
        "lru_b_x": nrm(ks[8], (DEPTH, 2, LRU_WIDTH), 0.02),
        "lru_lambda": jnp.log(lam_base) - jnp.log1p(-lam_base),
        "gmlp_ln_g": 1.0 + nrm(ks[11], (DEPTH, GMLP_WIDTH), 0.02),
        "gmlp_ln_b": nrm(ks[12], (DEPTH, GMLP_WIDTH), 0.02),
        "gmlp_w_s": nrm(ks[13], (DEPTH, GMLP_HEADS, CHUNK, CHUNK), 0.5 * CHUNK ** -0.5),
        "gmlp_b_s": 1.0 + nrm(ks[14], (DEPTH, GMLP_HEADS, CHUNK), 0.1),
        "w_out": nrm(ks[15], (DEPTH, MIX_WIDTH, D_MODEL), MIX_WIDTH ** -0.5),
        "ffn_norm_g": 1.0 + nrm(ks[16], (DEPTH, D_MODEL), 0.02),
        "peer_w_q": nrm(ks[17], (DEPTH, D_MODEL, PEER_HEADS * PEER_QDIM), D_MODEL ** -0.5),
        "peer_sub_keys": nrm(ks[18], (DEPTH, PEER_HEADS, 2, PEER_KEYS, PEER_HALF), PEER_HALF ** -0.5),
        "peer_u": nrm(ks[19], (DEPTH, PEER_EXPERTS, D_MODEL), D_MODEL ** -0.5),
        "peer_v": nrm(ks[20], (DEPTH, PEER_EXPERTS, D_MODEL), PEER_HEADS ** -0.5),
        "final_norm_g": 1.0 + nrm(ks[21], (D_MODEL,), 0.02),
    }

def second_block(x, mix_norm_g, w_in, conv_w, conv_b, lru_w_a, lru_b_a, lru_w_x, lru_b_x, lru_lambda,
              gmlp_ln_g, gmlp_ln_b, gmlp_w_s, gmlp_b_s, w_out, ffn_norm_g, peer_w_q, peer_sub_keys,
              peer_u, peer_v, final_norm_g):
    h = x
    for l in range(DEPTH):
        n = rms_norm(h, mix_norm_g[l])
        z = n @ w_in[l]
        xr = z[..., :LRU_WIDTH]
        gr = z[..., LRU_WIDTH:2 * LRU_WIDTH]
        gu = z[..., 2 * LRU_WIDTH:2 * LRU_WIDTH + GMLP_WIDTH]
        gv = z[..., 2 * LRU_WIDTH + GMLP_WIDTH:]
        a_out = recurrent_group(xr, gr, conv_w[l], conv_b[l], lru_w_a[l], lru_b_a[l],
                                lru_w_x[l], lru_b_x[l], lru_lambda[l])
        b_out = spatial_gating_group(gu, gv, gmlp_ln_g[l], gmlp_ln_b[l], gmlp_w_s[l], gmlp_b_s[l])
        h = h + jnp.concatenate([a_out, b_out], axis=-1) @ w_out[l]
        h = h + peer(rms_norm(h, ffn_norm_g[l]), peer_w_q[l], peer_sub_keys[l], peer_u[l], peer_v[l])
    return rms_norm(h, final_norm_g)


def setup_inputs(seed=0):
    out = dict(first_inputs(seed))
    for name, value in second_inputs(seed + 1).items():
        if name != "x":
            out[name + "_2"] = value
    return out


def reference(
    x, norm1_g, w_in, hg_lb_param, hg_norm_g, w_proj_a, w_proj_b, w_out, norm2_g, w_up, conv_w,
    conv_b, w_down, norm_f_g, mix_norm_g_2, w_in_2, conv_w_2, conv_b_2, lru_w_a_2, lru_b_a_2,
    lru_w_x_2, lru_b_x_2, lru_lambda_2, gmlp_ln_g_2, gmlp_ln_b_2, gmlp_w_s_2, gmlp_b_s_2,
    w_out_2, ffn_norm_g_2, peer_w_q_2, peer_sub_keys_2, peer_u_2, peer_v_2, final_norm_g_2,
):
    x = first_block(
        x, norm1_g, w_in, hg_lb_param, hg_norm_g, w_proj_a, w_proj_b, w_out, norm2_g, w_up,
        conv_w, conv_b, w_down, norm_f_g,
    )
    return second_block(
        x, mix_norm_g_2, w_in_2, conv_w_2, conv_b_2, lru_w_a_2, lru_b_a_2, lru_w_x_2, lru_b_x_2,
        lru_lambda_2, gmlp_ln_g_2, gmlp_ln_b_2, gmlp_w_s_2, gmlp_b_s_2, w_out_2, ffn_norm_g_2,
        peer_w_q_2, peer_sub_keys_2, peer_u_2, peer_v_2, final_norm_g_2,
    )


_drawn_inputs = setup_inputs


def setup_inputs(seed=0):
    import zlib

    import numpy as np

    out = dict(_drawn_inputs(seed))
    spreads = {}
    factors = {'hg_norm_g': 3.499,
     'conv_b': 2.867,
     'lru_b_a_2': 33.788,
     'lru_b_x_2': 20.991,
     'gmlp_ln_g_2': 13.557,
     'gmlp_ln_b_2': 14.663,
     'final_norm_g_2': 7.974,
     'norm2_g': 2.683,
     'ffn_norm_g_2': 3.425}
    for name, (base, spread) in spreads.items():
        noise = np.random.default_rng([zlib.crc32(name.encode()), seed]).standard_normal(out[name].shape)
        drawn = base * np.exp(spread * noise) if base else spread * noise
        out[name] = __import__('jax').numpy.asarray(drawn.astype(out[name].dtype))
    for name, factor in factors.items():
        out[name] = (out[name] * factor).astype(out[name].dtype)
    return out
```

```python
import math
from contextlib import ExitStack

import numpy as np
import concourse.bass as bass
from concourse import mybir

F32 = mybir.dt.float32
F32R = mybir.dt.float32r
U32 = mybir.dt.uint32
ALU = mybir.AluOpType
ACT = mybir.ActivationFunctionType
AX = mybir.AxisListType.X

P = 128
T = 256
D = 2048
FF = 5632
EPS = 1e-6
NEG = -1e30
SCALE = 128.0 ** -0.5

NR = 3
NS = 4
LOOK = 3
NU = 6
NV = 8
VLAG = 18


class Lane:

    def __init__(self, sem):
        self.sem, self.n, self.ops, self.met = sem, 0, [], {}

    def wait(self, *after):
        for t in flat(after):
            sem, v = t
            if self.met.get(id(sem), 0) < v:
                self.met[id(sem)] = v
                self.ops.append(lambda e, sem=sem, v=v: e.wait_ge(sem, v))

    def do(self, fn, *after, sig=True):
        self.wait(*after)
        if not sig:
            self.ops.append(fn)
            return None
        self.n += 1
        self.ops.append(lambda e: fn(e).then_inc(self.sem, 1))
        return (self.sem, self.n)

    def dma(self, fn, counter, *after):
        self.wait(*after)
        counter.n += 16
        self.ops.append(lambda e: fn(e).then_inc(counter.sem, 16))
        return (counter.sem, counter.n)

    def now(self):
        return (self.sem, self.n) if self.n else None

    def run(self, e):
        for op in self.ops:
            op(e)


class Counter:
    def __init__(self, sem):
        self.sem, self.n = sem, 0


class Bank:
    def __init__(self, t):
        self.t, self.free, self.held = t, [], False


def flat(x):
    for y in x:
        if y is None:
            continue
        if isinstance(y, list):
            yield from flat(y)
        else:
            yield y


def strided(a, *dims):
    return bass.AP(tensor=a.tensor, offset=a.offset, ap=[list(a.ap[0])] + [list(d) for d in dims])


def cat(*parts):
    return list(parts)


CONST = {}
_o = 0
for _n, _w in (("ident", 128), ("cos", 256), ("sin", 256), ("amask", 1536), ("hmask", 1024), ("iota", 16)):
    CONST[_n] = (_o, _w)
    _o += _w
CONST_W = _o


def shape_constants():
    c = np.zeros((P, CONST_W), np.float32)

    def put(name, v):
        o, w = CONST[name]
        c[:, o:o + w] = v.reshape(P, w)

    put("ident", np.eye(P, dtype=np.float32))
    half = 64
    inv = np.exp(np.float32(-math.log(10000.0)) * np.arange(half, dtype=np.float32) * np.float32(2.0 / 128))
    ang = np.arange(T, dtype=np.float32)[:, None] * inv.astype(np.float32)[None, :]
    co, si = np.cos(ang).astype(np.float32), np.sin(ang).astype(np.float32)
    put("cos", np.concatenate([co, co], 1).reshape(2, P, 128).transpose(1, 0, 2))
    put("sin", np.concatenate([-si, si], 1).reshape(2, P, 128).transpose(1, 0, 2))
    t, s = np.arange(T)[:, None], np.arange(T)[None, :]
    m = np.zeros((3, T, T), np.float32)
    for g, dil in enumerate((1, 4, 16)):
        ok = (t >= s) & ((t - s) % dil == 0) & (t - s <= 128 * dil)
        m[g] = np.where(ok, 0.0, NEG)
    put("amask", m.reshape(3, 2, P, T).transpose(2, 1, 0, 3))
    s, t = np.arange(P)[:, None], np.arange(P)[None, :]
    h = np.zeros((P, 8, P), np.float32)
    for lv in range(7):
        w = 1 << lv
        h[:, lv] = (s // (2 * w) == t // (2 * w)) & (s % (2 * w) < w) & (t % (2 * w) >= w)
    h[:, 7] = s == t
    put("hmask", h)
    put("iota", np.tile(np.arange(16, dtype=np.float32), (P, 1)))
    return c


def program(nc, io, out):
    with ExitStack() as ctx:
        def sem(name):
            return ctx.enter_context(nc.semaphore(name))

        SP, PE, AC, DV, PO = (Lane(sem(f"lane_{n}")) for n in ("sp", "pe", "act", "dve", "pool"))

        BASE = 16512
        top = [BASE]

        def at(name, shape, offset, dt=F32):
            return nc.alloc_sbuf_tensor_at(name, [P] + list(shape), dt, offset=offset)

        def low(name, shape, dt=F32):
            n = int(np.prod(shape)) * 4
            t = at(name, shape, top[0], dt)
            top[0] += (n + 31) // 32 * 32
            return t

        class Area:
            def __init__(self, start, end):
                self.o, self.end = start, end

            def get(self, name, shape, dt=F32):
                t = at(name, shape, self.o, dt)
                self.o += (int(np.prod(shape)) * 4 + 31) // 32 * 32
                assert self.o <= self.end, (name, self.o, self.end)
                return t

        ident = low("ident", [128])
        cst1 = low("cst1", [64])
        cst2 = low("cst2", [128])
        cw = low("cw", [4, 88])
        iota = low("iota", [16])
        ones = low("ones", [256])
        hgn = low("hgn", [128])
        eps = low("eps", [1])
        lb = low("lb", [16])
        oml = low("oml", [16])
        st6 = low("st6", [2, 4, 6])
        mv = low("mv", [2, 2])
        ms = low("ms", [2])
        sq = low("sq", [2])
        rstd = low("rstd", [2])
        nsp = low("nsp", [16])
        psp = low("psp", [16])
        diag = low("diag", [4, 128])
        X = low("X", [2, D])
        u0 = top[0]
        uh = low("uh", [16, T], F32R)
        ul = low("ul", [16, T], F32R)
        raw = low("raw", [NR, 2048])
        wh = low("wh", [NS, 1024], F32R)
        wl = low("wl", [NS, 1024], F32R)
        Z = top[0]
        END = 229344
        bank_names = ["W0", "W1", "W2", "W3", "T0", "T1", "M0", "M1"]
        W0, W1, W2, W3, T0, T1, M0, M1 = (
            Bank(ctx.enter_context(nc.psum_tensor(n, [P, 512], F32))) for n in bank_names)
        pairs = [(W0, W1), (W2, W3)]

        def act(o, i, f, *after, **kw):
            return AC.do(lambda e: e.activation(o, i, f, **kw), *after)

        def tt(o, a, b, op, *after, lane=None):
            return (lane or DV).do(lambda e: e.tensor_tensor(o, a, b, op), *after)

        def ts(o, a, s1, s2, op0, op1, *after, lane=None):
            if op1 is None:
                return (lane or DV).do(lambda e: e.tensor_scalar(o, a, s1, None, op0), *after)
            return (lane or DV).do(lambda e: e.tensor_scalar(o, a, s1, s2, op0, op1), *after)

        def stt(o, a, s, b, op0, op1, *after):
            return DV.do(lambda e: e.scalar_tensor_tensor(o, a, s, b, op0, op1), *after)

        def cp(o, i, *after):
            return DV.do(lambda e: e.tensor_copy(o, i), *after)

        def mm(o, l, r, start, stop, *after, sig=False):
            return PE.do(lambda e: e.matmul(o, l, r, start=start, stop=stop), *after, sig=sig)

        def tr(o, i, *after, sig=False, n=P):
            return PE.do(lambda e: e.transpose(o, i, ident[0:n, 0:n]), *after, sig=sig)

        def load(lane, o, i, name, *after):
            return lane.dma(lambda e: e.dma_start(o, i), Counter(sem(name)), *after)

        def fence():
            t = [PE.now(), AC.now(), DV.now(), PO.now()]
            for lane in (AC, DV, PO):
                lane.wait(t)
            return t

        A_, S_, M_ = ALU.add, ALU.subtract, ALU.mult

        def wide(w, c0, kt):
            return dict(kind="n", kt=kt, kc=4, n=512,
                        src=w[:, c0:c0 + 512].rearrange("(k p) n -> p k n", p=P))

        def tall(w, c0, kt):
            return dict(kind="s", kt=kt, kc=8, n=256,
                        src=w[:, c0:c0 + 256].rearrange("(k p) n -> p k n", p=P))

        w_in, w_pa, w_pb, w_out = io["w_in"][0], io["w_proj_a"][0], io["w_proj_b"][0], io["w_out"][0]
        w_up, w_down = io["w_up"][0], io["w_down"][0]
        w_in2, w_out2, w_q = io["w_in_2"][0], io["w_out_2"][0], io["peer_w_q_2"][0]
        blocks = []
        for base in (11264, 9728, 8192):
            blocks += [wide(w_in, base + 512 * g, 16) for g in range(3)]
        for g in range(4):
            blocks += [wide(w_in, 4096 + 512 * g, 16), wide(w_in, 6144 + 512 * g, 16)]
            blocks += [tall(w_in, b + 512 * g + 256 * i, 16) for b in (0, 2048) for i in range(2)]
        for n in range(4):
            blocks += [wide(w_in, 12800 + 512 * n, 16), wide(w_pa, 512 * n, 16),
                       wide(w_in, 14848 + 512 * n, 16), wide(w_pb, 512 * n, 4)]
        blocks += [wide(w_out, 512 * n, 16) for n in range(4)]
        for j in range(22):
            blocks += [tall(w_up, 256 * j, 16), tall(w_up, FF + 256 * j, 16)]
        blocks += [wide(w_down, 512 * n, 44) for n in range(4)]
        blocks += [tall(w_in2, 256 * j, 16) for j in range(8)]
        blocks += [wide(w_in2, c, 16) for c in (3072, 3584, 2048, 2560)]
        blocks += [wide(w_out2, 512 * n, 16) for n in range(4)]
        blocks += [tall(w_q, 256 * j, 16) for j in range(8)]

        chunks, subs = [], []
        for b in blocks:
            b["first"] = len(subs)
            for c in range(b["kt"] // b["kc"]):
                chunks.append((b, c * b["kc"]))
                for half in range(2):
                    subs.append((b, c * b["kc"] + half * (b["kc"] // 2), len(chunks) - 1, half))
        raw_sems = [Counter(sem(f"raw{i}")) for i in range(NR)]
        landed, split, used = {}, {}, {}

        def fetch(c):
            b, k0 = chunks[c]
            dst = raw[:, c % NR, :].rearrange("p (k n) -> p k n", n=b["n"])
            src = b["src"][:, k0:k0 + b["kc"], :]
            after = split[2 * (c - NR) + 1] if c >= NR else None
            landed[c] = SP.dma(lambda e: e.dma_start(dst, src), raw_sems[c % NR], after)

        conv_at = [0]

        def convert_upto(s_end):
            while conv_at[0] < min(s_end, len(subs)):
                s = conv_at[0]
                _, _, c, half = subs[s]
                r = raw[:, c % NR, half * 1024:(half + 1) * 1024]
                ta = act(wh[:, s % NS, :], r, ACT.Copy, landed[c], used.get(s - NS))
                split[s] = tt(wl[:, s % NS, :], r, wh[:, s % NS, :].bitcast(F32), S_, ta, used.get(s - NS))
                if half == 1 and c + NR < len(chunks):
                    fetch(c + NR)
                conv_at[0] += 1

        tasks = []
        ACTIVE = 2

        def step():
            if tasks:
                g = tasks.pop(0)
                try:
                    next(g)
                    tasks.insert(min(ACTIVE - 1, len(tasks)), g)
                except StopIteration:
                    pass

        def drain():
            while tasks:
                step()

        block_at = [0]

        def stream(xh, xl, ready, steps=1):
            b = blocks[block_at[0]]
            pr = pairs[block_at[0] % 2]
            block_at[0] += 1
            n_sub = 2 * (b["kt"] // b["kc"])
            for i in range(n_sub):
                s = b["first"] + i
                convert_upto(s + 1 + LOOK)
                _, k0, _, _ = subs[s]
                kc = b["kc"] // 2
                H = wh[:, s % NS, :].rearrange("p (k n) -> p k n", n=b["n"])
                L = wl[:, s % NS, :].rearrange("p (k n) -> p k n", n=b["n"])
                PE.wait(split[s])
                if i == 0:
                    PE.wait(pr[0].free, pr[1].free)
                for k in range(kc):
                    kk = k0 + k
                    PE.wait(ready[kk])
                    first, last = kk == 0, kk == b["kt"] - 1
                    for h in range(2):
                        end = k == kc - 1 and h == 1
                        if b["kind"] == "n":
                            o = pr[h].t[:, :]
                            th, tl = xh[:, kk, h * P:(h + 1) * P], xl[:, kk, h * P:(h + 1) * P]
                            mm(o, th, H[:, k, :], first, False)
                            mm(o, th, L[:, k, :], False, False)
                            t = mm(o, tl, H[:, k, :], False, last, sig=end)
                        else:
                            o = pr[h].t[:, 0:T]
                            vh, vl = H[:, k, h * P:(h + 1) * P], L[:, k, h * P:(h + 1) * P]
                            mm(o, vh, xh[:, kk, :], first, False)
                            mm(o, vh, xl[:, kk, :], False, False)
                            t = mm(o, vl, xh[:, kk, :], False, last, sig=end)
                used[s] = t
                for _ in range(steps):
                    step()
            return pr, t

        def hold(*bs):
            while any(b.held for b in bs):
                yield
            for b in bs:
                b.held = True

        def stats(t, j, src, *after):
            return DV.do(lambda e: e.bn_stats(st6[:, t, j, :], src), *after)

        def finish_stats(t, n, *after):
            a = DV.do(lambda e: e.bn_aggr(mv[:, t, :], st6[:, t, 0:n, :].rearrange("p a b -> p (a b)")), *after)
            return a

        def rms(t, *after):
            a = finish_stats(t, 4, *after)
            m = stt(ms[:, t:t + 1], mv[:, t, 0:1], mv[:, t, 0:1], mv[:, t, 1:2], M_, A_, a)
            s = act(sq[:, t:t + 1], ms[:, t:t + 1], ACT.Sqrt, m, bias=eps[:, 0:1])
            return DV.do(lambda e: e.reciprocal(rstd[:, t:t + 1], sq[:, t:t + 1]), s)

        def to_uT(piece, gcol, ready_in, after_pe, ks=range(0, 16, 2)):
            ready = {}
            for k in ks:
                bk = (T0, T1)[(k // 2) % 2]
                for kk in (k, k + 1):
                    for t in range(2):
                        o = bk.t[:, (kk - k) * T + t * P:(kk - k) * T + (t + 1) * P]
                        tk = tr(o, piece(t, kk), ready_in(t, kk), bk.free, sig=(kk == k + 1 and t == 1))
                if gcol is None:
                    a = act(uh[:, k:k + 2, :], bk.t[:, :].rearrange("p (k t) -> p k t", k=2), ACT.Copy, tk, after_pe)
                    d = tt(ul[:, k:k + 2, :], bk.t[:, :].rearrange("p (k t) -> p k t", k=2),
                           uh[:, k:k + 2, :].bitcast(F32), S_, a, after_pe)
                    ready[k] = ready[k + 1] = d
                else:
                    for kk in (k, k + 1):
                        v = bk.t[:, (kk - k) * T:(kk - k + 1) * T]
                        a = act(uh[:, kk, :], v, ACT.Copy, tk, after_pe, scale=gcol(kk))
                    for kk in (k, k + 1):
                        v = bk.t[:, (kk - k) * T:(kk - k + 1) * T]
                        d = stt(ul[:, kk, :], v, gcol(kk), uh[:, kk, :].bitcast(F32), M_, S_, a, after_pe)
                        ready[kk] = d
                bk.free = [a, d]
            return ready

        def scaled(xs, src_after):
            r = [rms(t, src_after[t]) for t in range(2)]
            out = {}
            for j in range(4):
                c = slice(512 * j, 512 * (j + 1))
                out[0, j] = act(xs[:, 0, c], X[:, 0, c], ACT.Copy, r[0], scale=rstd[:, 0:1])
                out[1, j] = ts(xs[:, 1, c], X[:, 1, c], rstd[:, 1:2], None, M_, None, r[1])
            return out

        def normed(xs, src_after, gcol, after_pe):
            ok = scaled(xs, src_after)
            return to_uT(lambda t, k: xs[:, t, k * P:(k + 1) * P], gcol, lambda t, k: ok[t, k // 4], after_pe)

        con = io["consts"]

        def cslice(n):
            o, w = CONST[n]
            return con[:, o:o + w]

        x_dram = io["x"][0].rearrange("(t p) d -> p t d", p=P)
        tx = [load(SP, X[:, t, :], x_dram[:, t, :], f"x{t}") for t in range(2)]
        t_id = load(AC, ident[:, :], cslice("ident"), "c_id")
        st_area = Area(Z, END)
        xs = st_area.get("xs_a", [2, D])
        st1 = st_area.get("st1", [128])
        st2 = st_area.get("st2", [128])
        cws = st_area.get("cws", [4, 128])
        lbt = st_area.get("lbt", [16])
        c1 = Counter(sem("c_st1"))
        c2 = Counter(sem("c_st2"))
        c3 = Counter(sem("c_cw"))

        def rows(dst, r0, src, counter):
            n = src.shape[0]
            return AC.dma(lambda e: e.dma_start(dst[r0:r0 + n, :], src), counter)

        rows(st1, 0, io["norm1_g"].rearrange("o (k p) -> (o k) p", p=P), c1)
        rows(st1, 16, io["norm2_g"].rearrange("o (k p) -> (o k) p", p=P), c1)
        t_st1 = rows(st1, 32, io["hg_lb_param"].rearrange("o (k p) -> (o k) p", p=P), c1)
        for r0, nm in ((0, "mix_norm_g_2"), (16, "ffn_norm_g_2"), (80, None)):
            if nm:
                rows(st2, r0, io[nm].rearrange("o (k p) -> (o k) p", p=P), c2)
        rows(st2, 32, io["conv_w_2"][0].rearrange("o (k p) -> (o k) p", p=P), c2)
        rows(st2, 64, io["conv_b_2"].rearrange("o (k p) -> (o k) p", p=P), c2)
        rows(st2, 72, io["gmlp_b_s_2"][0], c2)
        rows(st2, 80, io["lru_b_a_2"][0].rearrange("o (k p) -> (o k) p", p=P), c2)
        rows(st2, 96, io["lru_b_x_2"][0].rearrange("o (k p) -> (o k) p", p=P), c2)
        t_st2 = rows(st2, 112, io["lru_lambda_2"][0].rearrange("o (k p) -> (o k) p", p=P), c2)
        AC.dma(lambda e: e.dma_start(cws[0:88, 0:3, :], io["conv_w"][0].rearrange("o (k p) -> k o p", p=P)), c3)
        t_cw = AC.dma(lambda e: e.dma_start(cws[0:88, 3, :], io["conv_b"][0].rearrange("(k p) -> k p", p=P)), c3)
        t_hgn = load(AC, hgn[:, :], io["hg_norm_g"][0].partition_broadcast(P), "c_hgn")
        t_io = load(AC, iota[:, :], cslice("iota"), "c_iota")
        t_ones = PO.do(lambda e: e.memset(ones[:, :], 1.0))
        t_eps = PO.do(lambda e: e.memset(eps[:, :], EPS))
        AC.wait(t_eps)
        for c in range(NR):
            fetch(c)

        ss = [[stats(t, j, X[:, t, 512 * j:512 * (j + 1)], tx[t]) for j in range(4)] for t in range(2)]
        k1 = tr(M0.t[:, 0:64], st1[0:64, :], t_st1, t_id, n=64)
        k2 = tr(M0.t[:, 64:192], st2[:, :], t_st2, sig=True)
        for o in range(4):
            k3 = tr(M1.t[:, 88 * o:88 * o + 88], cws[0:88, o, :], t_cw, sig=(o == 3), n=88)
        q1 = cp(cst1[:, :], M0.t[:, 0:64], k2)
        q2 = cp(cst2[:, :], M0.t[:, 64:192], k2)
        q3 = cp(cw[:, :, :], M1.t[:, 0:352].rearrange("p (o k) -> p o k", o=4), k3)
        M0.free, M1.free = [q1, q2], [q3]
        AC.wait(q1, q2, q3)
        l1 = tt(lbt[:, :], cst1[:, 32:48], cst1[:, 48:64], S_, q1)
        t_lb = [act(lb[:, :], lbt[:, :], ACT.Sigmoid, l1), act(oml[:, :], lbt[:, :], ACT.Sigmoid, l1, scale=-1.0)]
        DV.wait(t_lb, q1, q2, q3)
        lam = cst2[:, 112:128]
        sa = [st_area.get(f"sp{i}", [16]) for i in range(5)]
        z = ts(sa[0][:, :], lam, -1.0, None, M_, None)
        z = tt(sa[0][:, :], lam, sa[0][:, :], ALU.min, z)
        z = act(sa[1][:, :], sa[0][:, :], ACT.Exp, z)
        z = ts(sa[2][:, :], sa[1][:, :], 2.0, None, A_, None, z)
        z = DV.do(lambda e: e.reciprocal(sa[3][:, :], sa[2][:, :]), z)
        z = tt(sa[2][:, :], sa[1][:, :], sa[3][:, :], M_, z)
        z = tt(sa[3][:, :], sa[2][:, :], sa[2][:, :], M_, z)
        z = ts(sa[4][:, :], sa[3][:, :], 2.0 / 17, 2.0 / 15, M_, A_, z)
        for c in (13, 11, 9, 7, 5, 3, 1):
            z = tt(sa[4][:, :], sa[4][:, :], sa[3][:, :], M_, z)
            z = ts(sa[4][:, :], sa[4][:, :], 2.0 / c, None, A_, None, z)
        z = tt(sa[4][:, :], sa[4][:, :], sa[2][:, :], M_, z)
        z1 = ts(sa[0][:, :], lam, -1.0, 0.0, M_, ALU.max, z)
        z = tt(sa[4][:, :], sa[4][:, :], sa[0][:, :], A_, z, z1)
        ts(nsp[:, :], sa[4][:, :], -8.0, None, M_, None, z)
        t_nsp = ts(psp[:, :], sa[4][:, :], 8.0, None, M_, None, z)
        AC.wait(t_nsp)

        ready = normed(xs, ss, lambda k: cst1[:, k:k + 1], None)
        ready = [ready[k] for k in range(16)]

        area = Area(Z, END)
        obh = area.get("obh", [4, T], F32R)
        obl = area.get("obl", [4, T], F32R)
        qb = area.get("qb", [4, T])
        kb = area.get("kb", [4, T])
        Gb = area.get("Gb", [4, T])
        vb = [area.get(f"vb{i}", [2, 512]) for i in range(2)]
        gb = [area.get(f"gb{i}", [2, 512]) for i in range(2)]
        Z2 = area.o
        fz = fence()
        area = Area(Z2, END)
        qT = area.get("qT", [12, T])
        kT = area.get("kT", [12, T])
        vA = area.get("vA", [2, 1536])
        Sb = [area.get(f"S{i}", [768]) for i in range(2)]
        pT = area.get("pT", [6, P])
        r1 = area.get("r1", [512])
        r2 = [area.get(f"r2{i}", [512]) for i in range(2)]
        cos = area.get("cosT", [2, 128])
        sin = area.get("sinT", [2, 128])
        amask = area.get("amask", [2, 3, T])
        sm = area.get("sm", [8, 4])
        t_cos = load(PO, cos[:, :, :], cslice("cos").rearrange("p (t d) -> p t d", t=2), "c_cos", fz)
        t_sin = load(PO, sin[:, :, :], cslice("sin").rearrange("p (t d) -> p t d", t=2), "c_sin", fz)
        t_am = load(PO, amask[:, :, :, :], cslice("amask").rearrange("p (t g s) -> p t g s", t=2, g=3), "c_am", fz)

        for g in range(3):
            pr, t = stream(uh, ul, ready)
            for i in range(2):
                pr[i].free = [act(vA[:, i, 512 * g:512 * (g + 1)], pr[i].t[:, :], ACT.Copy, t)]
        t_v = AC.now()
        r2_free = [[], []]
        rope_t = []
        for dst in (kT, qT):
            for g in range(3):
                pr, t = stream(uh, ul, ready)
                for i in range(2):
                    pv = pr[i].t[:, :].rearrange("p (h d) -> p h d", h=4)
                    v1 = r1[:, :].rearrange("p (h d) -> p h d", h=4)
                    v2 = r2[i][:, :].rearrange("p (h d) -> p h d", h=4)
                    a = tt(v1, pv, strided(cos[:, i, :], [0, 4], [1, 128]), M_, t, t_cos, DV.now())
                    b = tt(v2[:, :, 0:64], pv[:, :, 64:128], strided(sin[:, i, 0:64], [0, 4], [1, 64]), M_, t_sin, r2_free[i])
                    c = tt(v2[:, :, 64:128], pv[:, :, 0:64], strided(sin[:, i, 64:128], [0, 4], [1, 64]), M_)
                    pr[i].free = [c]
                    d = tt(r2[i][:, :], r1[:, :], r2[i][:, :], A_, a, b, c)
                    bk = (T0, T1)[i]
                    for h in range(4):
                        tk = tr(bk.t[:, h * P:(h + 1) * P], r2[i][:, h * P:(h + 1) * P], d, bk.free, sig=(h == 3))
                    r2_free[i] = [tk]
                    e = act(dst[:, 4 * g:4 * g + 4, i * P:(i + 1) * P],
                            bk.t[:, :].rearrange("p (h t) -> p h t", h=4), ACT.Copy, tk)
                    bk.free = [e]
                    rope_t = [e]

        s_free, p_free, ob_t = [[], []], [[]], []

        def attend(n, hg, t):
            ns = 1 + t
            w = P * ns
            S = Sb[n % 2]
            sv = S[:, 0:3 * w].rearrange("p (g s) -> p g s", g=3)
            yield from hold(M0, M1)
            for g in range(3):
                o = M0.t[:, g * w:(g + 1) * w] if (t == 0 or g < 2) else M1.t[:, 0:w]
                tk = mm(o, qT[:, 4 * g + hg, t * P:(t + 1) * P], kT[:, 4 * g + hg, 0:w], True, True,
                        rope_t, t_v, M0.free, M1.free, sig=(g == 2))
            yield
            if t == 0:
                d = tt(sv, M0.t[:, 0:3 * w].rearrange("p (g s) -> p g s", g=3), amask[:, 0, :, 0:w], A_, tk, t_am, s_free[n % 2])
                dd = [d]
            else:
                d1 = tt(sv[:, 0:2, :], M0.t[:, :].rearrange("p (g s) -> p g s", g=2), amask[:, 1, 0:2, :], A_, tk, t_am, s_free[n % 2])
                d2 = tt(sv[:, 2, :], M1.t[:, 0:w], amask[:, 1, 2, :], A_)
                dd = [d1, d2]
            M0.free = M1.free = dd
            M0.held = M1.held = False
            m = DV.do(lambda e: e.tensor_reduce(sm[:, n, 0:1], S[:, 0:3 * w], AX, ALU.max), dd)
            m = ts(sm[:, n, 1:2], sm[:, n, 0:1], -SCALE, None, M_, None, m)
            yield
            a = act(S[:, 0:3 * w], S[:, 0:3 * w], ACT.Exp, m, dd, scale=SCALE, bias=sm[:, n, 1:2], accum_out=sm[:, n, 2:3])
            yield
            r = DV.do(lambda e: e.reciprocal(sm[:, n, 3:4], sm[:, n, 2:3]), a)
            r = ts(S[:, 0:3 * w], S[:, 0:3 * w], sm[:, n, 3:4], None, M_, None, r)
            yield from hold(T0, T1)
            nb = 3 * ns
            for j in range(nb):
                bk, c = (T0, j) if j < 4 else (T1, j - 4)
                tk = tr(bk.t[:, c * P:(c + 1) * P], S[:, j * P:(j + 1) * P], r, bk.free, sig=(j == nb - 1))
            s_free[n % 2] = [tk]
            yield
            n0 = min(nb, 4)
            e1 = act(pT[:, 0:n0, :], T0.t[:, 0:n0 * P].rearrange("p (j t) -> p j t", t=P), ACT.Copy, tk, p_free[0])
            e2 = cp(pT[:, 4:6, :], T1.t[:, 0:2 * P].rearrange("p (j t) -> p j t", t=P), tk, p_free[0]) if nb > 4 else None
            T0.free, T0.held = [e1], False
            yield
            o = T1.t[:, 256:384]
            for j in range(nb):
                g, si = j // ns, j % ns
                tk = mm(o, vA[:, si, (4 * g + hg) * P:(4 * g + hg + 1) * P], pT[:, j, :], j == 0, j == nb - 1,
                        e1, e2, T1.free, sig=(j == nb - 1))
            p_free[0] = [tk]
            yield
            a = act(obh[:, hg, t * P:(t + 1) * P], o, ACT.Copy, tk)
            d = tt(obl[:, hg, t * P:(t + 1) * P], o, obh[:, hg, t * P:(t + 1) * P].bitcast(F32), S_, a)
            T1.free, T1.held = [e2, a, d], False
            ob_t[:] = [d]

        for n in range(8):
            tasks.append(attend(n, n // 2, n % 2))

        hg_mem = {}

        def hg_setup():
            drain()
            fz = fence()
            area = Area(Z2, END)
            hg_mem["oah"] = area.get("oah", [16, T], F32R)
            hg_mem["oal"] = area.get("oal", [16, T], F32R)
            hg_mem["E"] = [area.get(f"E{i}", [8, T]) for i in range(2)]
            hg_mem["prod"] = area.get("prod", [8, P])
            hg_mem["mask"] = area.get("hmask", [8, P])
            hg_mem["AT"] = [area.get(f"AT{i}", [3, P]) for i in range(2)]
            hg_mem["o"] = area.get("o_n", [2, P])
            hg_mem["junk"] = area.get("junk", [P])
            hg_mem["s"] = area.get("hs", [2, 2, 4])
            hg_mem["t_mask"] = load(PO, hg_mem["mask"][:, :, :], cslice("hmask").rearrange("p (l t) -> p l t", l=8), "c_hm", fz)

        E_free, AT_free, o_free, prod_free = [[], []], [[], []], [[]], [[]]
        grp_done = [[]]
        vg_done = [[], []]

        def halves(E, lv):
            w = 1 << lv
            v = E[:, lv, :].rearrange("p (b c) -> p b c", c=2 * w)
            return v[:, :, 0:w], v[:, :, w:2 * w]

        def scan_head(g, j, t_lnf):
            hd = 4 * g + j
            E, AT = hg_mem["E"][j % 2], hg_mem["AT"][j % 2]
            prod, mask, on, junk, hs = (hg_mem[k] for k in ("prod", "mask", "o", "junk", "s"))
            oah, oal = hg_mem["oah"], hg_mem["oal"]
            G = Gb[:, j, :]
            c = DV.do(lambda e: e.tensor_tensor_scan(G, ones[:, :], G, 0.0, M_, A_), t_lnf, t_ones)
            for lv in range(8):
                w = 1 << lv
                gv = G.rearrange("p (b c) -> p b c", c=2 * w)
                ref = strided(G[:, w - 1:w], [2 * w, T // (2 * w)], [0, w])
                el, er = halves(E, lv)
                d1 = tt(el, ref, gv[:, :, 0:w], S_, c, E_free[j % 2])
                d2 = tt(er, gv[:, :, w:2 * w], ref, S_)
                if lv == 3:
                    yield
            yield
            a1 = act(E[:, 0:4, :], E[:, 0:4, :], ACT.Exp, d2)
            a2 = act(E[:, 4:8, :], E[:, 4:8, :], ACT.Exp, d2)
            yield
            for lv in range(8):
                w = 1 << lv
                el, er = halves(E, lv)
                kv = kb[:, j, :].rearrange("p (b c) -> p b c", c=2 * w)
                qv = qb[:, j, :].rearrange("p (b c) -> p b c", c=2 * w)
                m1 = tt(el, el, kv[:, :, 0:w], M_, a1 if lv < 4 else a2)
                m2 = tt(er, er, qv[:, :, w:2 * w], M_)
                if lv == 3:
                    yield
            for i in range(2):
                cs = slice(i * P, (i + 1) * P)
                yield from hold(M0, M1)
                for lv in range(8):
                    bk = M0 if lv < 4 else M1
                    o = bk.t[:, (lv % 4) * P:(lv % 4 + 1) * P]
                    if lv < 7:
                        tk = mm(o, E[:, lv, cs], E[:, lv, cs], True, True, m2, bk.free)
                    else:
                        tk = mm(o, kb[:, j, cs], qb[:, j, cs], True, True, sig=True)
                yield
                p1 = tt(prod[:, 0:4, :], M0.t[:, :].rearrange("p (l t) -> p l t", l=4), mask[:, 0:4, :], M_, tk, hg_mem["t_mask"], prod_free[0])
                p2 = tt(prod[:, 4:8, :], M1.t[:, :].rearrange("p (l t) -> p l t", l=4), mask[:, 4:8, :], M_)
                M0.free, M1.free = [p1], [p2]
                M0.held = M1.held = False
                s = DV.do(lambda e, i=i: e.tensor_reduce(AT[:, 2 * i, :], prod[:, :, :].rearrange("p l t -> p t l"), AX, A_), p1, p2, AT_free[j % 2])
                prod_free[0] = [s]
            yield from hold(T0)
            tk = mm(T0.t[:, 0:P], E[:, 7, 0:P], E[:, 7, P:T], True, True, T0.free, sig=True)
            E_free[j % 2] = [tk]
            yield
            a = act(AT[:, 1, :], T0.t[:, 0:P], ACT.Copy, tk, AT_free[j % 2])
            yield
            v0, v1 = vb[g % 2][:, 0, j * P:(j + 1) * P], vb[g % 2][:, 1, j * P:(j + 1) * P]
            mm(T0.t[:, P:2 * P], AT[:, 0, :], v0, True, True, s, a)
            mm(T0.t[:, 2 * P:3 * P], AT[:, 1, :], v0, True, False)
            tk = mm(T0.t[:, 2 * P:3 * P], AT[:, 2, :], v1, False, True, sig=True)
            AT_free[j % 2] = [tk]
            yield
            h2 = hs[:, j % 2, :, :]
            for i in range(2):
                a = act(junk[:, :], T0.t[:, (1 + i) * P:(2 + i) * P], ACT.Square, tk, AC.now(), accum_out=h2[:, i, 0:1])
            x_, y_, w_ = h2[:, :, 0], h2[:, :, 1], h2[:, :, 2]
            d = ts(x_, x_, 1.0 / P, EPS, M_, A_, a)
            a = act(y_, x_, ACT.Ln, d)
            a = act(y_, y_, ACT.Exp, a, scale=-0.5)
            yield
            d = tt(w_, y_, y_, M_, a)
            d = tt(w_, w_, x_, M_, d)
            d = ts(w_, w_, -0.5, 1.5, M_, A_, d)
            d = tt(y_, y_, w_, M_, d)
            for i in range(2):
                e = stt(on[:, i, :], T0.t[:, (1 + i) * P:(2 + i) * P], h2[:, i, 1:2], gb[g % 2][:, i, j * P:(j + 1) * P],
                        M_, M_, d, o_free[0])
            T0.free, T0.held = [e], False
            yield from hold(T1)
            for i in range(2):
                tk = tr(T1.t[:, i * P:(i + 1) * P], on[:, i, :], e, T1.free, sig=(i == 1))
            o_free[0] = [tk]
            yield
            a = act(oah[:, hd, :], T1.t[:, 0:T], ACT.Copy, tk)
            d = tt(oal[:, hd, :], T1.t[:, 0:T], oah[:, hd, :].bitcast(F32), S_, a)
            T1.free, T1.held = [a, d], False
            hg_mem["done"] = [d]
            if j == 3:
                grp_done[0] = [DV.now(), PE.now()]
                vg_done[g % 2] = [DV.now(), PE.now()]

        for g in range(4):
            steps = 2 if g == 0 else 1
            pr, t = stream(uh, ul, ready, steps)
            for i in range(2):
                pr[i].free = [act(vb[g % 2][:, i, :], pr[i].t[:, :], ACT.Copy, t, vg_done[g % 2])]
            t_vb = AC.now()
            pr, t = stream(uh, ul, ready, steps)
            for i in range(2):
                gv = gb[g % 2][:, i, :]
                a = act(gv, pr[i].t[:, :], ACT.Sigmoid, t, vg_done[g % 2])
                d = tt(gv, pr[i].t[:, :], gv, M_, a)
                pr[i].free = [d]
                t_gb = tt(gv.rearrange("p (h d) -> p h d", h=4), gv.rearrange("p (h d) -> p h d", h=4),
                          strided(hgn[:, :], [0, 4], [1, 128]), M_, d, t_hgn)
            if g > 0:
                drain()
            for b in range(2):
                pr, t = stream(uh, ul, ready, steps)
                for i in range(2):
                    o = qb[:, 2 * b + i, :]
                    a = act(o, pr[i].t[:, 0:T], ACT.Sigmoid, t, grp_done[0])
                    d = tt(o, pr[i].t[:, 0:T], o, M_, a)
                    pr[i].free = [d]
            for b in range(2):
                pr, t = stream(uh, ul, ready, steps)
                for i in range(2):
                    hh = 4 * g + 2 * b + i
                    f, k = Gb[:, 2 * b + i, :], kb[:, 2 * b + i, :]
                    a = act(f, pr[i].t[:, 0:T], ACT.Sigmoid, t, grp_done[0])
                    a2 = act(k, pr[i].t[:, 0:T], ACT.Sigmoid, scale=-1.0)
                    pr[i].free = [a2]
                    ts(k, k, oml[:, hh:hh + 1], None, M_, None, a2)
                    d = ts(f, f, oml[:, hh:hh + 1], lb[:, hh:hh + 1], M_, A_, a)
            t_ln = act(Gb[:, :, :], Gb[:, :, :], ACT.Ln, d)
            if g == 0:
                hg_setup()
            PE.wait(t_vb, t_gb)
            tasks += [scan_head(g, j, t_ln) for j in range(4)]

        m_area = Area(Z + 8192, END)

        def gates_memory():
            fence()
            mix = m_area.get("mix", [2, D])
            sg = m_area.get("sg", [2, 512])
            tmp = m_area.get("tmpm", [2, 512])
            return mix, sg, tmp

        pr, t = stream(uh, ul, ready, 2)
        drain()
        mix, sg, tmp = gates_memory()
        oah, oal = hg_mem["oah"], hg_mem["oal"]
        oa_ready = [hg_mem["done"]] * 16
        ob_ready = [ob_t[0]] * 4
        mt = {}
        for n in range(4):
            c = slice(512 * n, 512 * (n + 1))
            if n:
                pr, t = stream(uh, ul, ready)
            for i in range(2):
                pr[i].free = [act(sg[:, i, :], pr[i].t[:, :], ACT.Sigmoid, t, DV.now())]
            a = AC.now()
            pr, t = stream(oah, oal, oa_ready)
            for i in range(2):
                pr[i].free = [tt(mix[:, i, c], pr[i].t[:, :], sg[:, i, :], M_, t, a)]
            d0 = DV.now()
            pr, t_gate = stream(uh, ul, ready)
            for i in range(2):
                pr[i].free = [act(sg[:, i, :], pr[i].t[:, :], ACT.Sigmoid, t_gate, d0)]
            a = AC.now()
            pr, t = stream(obh, obl, ob_ready)
            for i in range(2):
                d = tt(tmp[:, i, :], pr[i].t[:, :], sg[:, i, :], M_, t, a, DV.now())
                pr[i].free = [d]
                mt[i, n] = tt(mix[:, i, c], mix[:, i, c], tmp[:, i, :], A_, d, d0)
        rm = to_uT(lambda t, k: mix[:, t, k * P:(k + 1) * P], None, lambda t, k: mt[t, k // 4], t_gate)
        ready = [rm[k] for k in range(16)]

        def residual(xh, xl, rdy, steps=1):
            ss = [[], []]
            for n in range(4):
                c = slice(512 * n, 512 * (n + 1))
                pr, t = stream(xh, xl, rdy, steps)
                for i in range(2):
                    d = tt(X[:, i, c], pr[i].t[:, :], X[:, i, c], A_, t)
                    pr[i].free = [d]
                    ss[i].append(stats(i, n, X[:, i, c], d))
            return ss

        ss = residual(uh, ul, ready)

        fence()
        area = Area(Z, END)
        xs = at("xs_b", [2, D], Z)
        rm = normed(xs, ss, lambda k: cst1[:, 16 + k:17 + k], PE.now())
        ready = [rm[k] for k in range(16)]
        fence()
        gh = area.get("gh", [44, T], F32R)
        gl = area.get("gl", [44, T], F32R)
        ya = [area.get(f"ya{i}", [2, T]) for i in range(2)]
        yb = [area.get(f"yb{i}", [2, T]) for i in range(2)]

        def conv3(pr, t, y, j0, y_free):
            for i in range(2):
                j = j0 + i
                p = pr[i].t
                a = act(y[:, i, :], p[:, 0:T], ACT.Identity, t, y_free, scale=cw[:, 2, j:j + 1], bias=cw[:, 3, j:j + 1])
                d = stt(y[:, i, 1:T], p[:, 0:T - 1], cw[:, 1, j:j + 1], y[:, i, 1:T], M_, A_, a)
                d = stt(y[:, i, 2:T], p[:, 0:T - 2], cw[:, 0, j:j + 1], y[:, i, 2:T], M_, A_, d)
                pr[i].free = [d]
            return DV.now()

        ya_free, yb_free = [[], []], [[], []]
        g_ready = []
        for j in range(22):
            a_, b_ = ya[j % 2], yb[j % 2]
            pr, t = stream(uh, ul, ready)
            d = conv3(pr, t, a_, 2 * j, ya_free[j % 2])
            a = act(a_[:, :, :], a_[:, :, :], ACT.Gelu_apprx_tanh, d)
            pr, t = stream(uh, ul, ready)
            d = conv3(pr, t, b_, 44 + 2 * j, yb_free[j % 2])
            d = tt(a_[:, :, :], a_[:, :, :], b_[:, :, :], M_, d, a)
            yb_free[j % 2] = [d]
            o = slice(2 * j, 2 * j + 2)
            a = act(gh[:, o, :], a_[:, :, :], ACT.Copy, d)
            d = tt(gl[:, o, :], a_[:, :, :], gh[:, o, :].bitcast(F32), S_, a)
            ya_free[j % 2] = [a, d]
            g_ready += [d, d]
        ss = residual(gh, gl, g_ready)
        fz = fence()

        area = Area(Z, END)
        xs = area.get("xs_c", [2, D])
        area.o = Z
        lt = [area.get(f"lt{i}", [4, T]) for i in range(4)]
        uN = area.get("uN", [2, 1024])
        vN = area.get("vN", [2, 1024])
        lng = area.get("lng", [1024])
        lnb = area.get("lnb", [1024])
        xc = area.get("xc", [8, T])
        ggr = area.get("ggr", [8, T])
        ho = area.get("ho", [8, T])
        lw = area.get("lw", [32, P])
        wsn = area.get("wsn", [8, P])
        wsT = area.get("wsT", [8, P])
        g1 = at("g1", [D], Z + 16384)
        t_g1 = load(AC, g1[:, :], io["norm_f_g"].partition_broadcast(P), "c_nf", fz)
        t_lw1 = load(PO, lw[:, 0:16, :], io["lru_w_a_2"][0].rearrange("d h c e -> c (d h) e"), "c_lwa", fz)
        t_lw2 = load(PO, lw[:, 16:32, :], io["lru_w_x_2"][0].rearrange("d h c e -> c (d h) e"), "c_lwx", fz)
        t_ws = load(PO, wsn[:, :, :], io["gmlp_w_s_2"][0].rearrange("h p q -> p h q"), "c_ws", fz)
        t_lng = load(PO, lng[:, :], io["gmlp_ln_g_2"][0].partition_broadcast(P), "c_lng", fz)
        t_lnb = load(PO, lnb[:, :], io["gmlp_ln_b_2"][0].partition_broadcast(P), "c_lnb", fz)
        r = [rms(t, ss[t]) for t in range(2)]
        ss = [[], []]
        for t in range(2):
            for j in range(4):
                c = slice(512 * j, 512 * (j + 1))
                d = stt(X[:, t, c], X[:, t, c], rstd[:, t:t + 1], g1[:, c], M_, M_, r[t], t_g1)
                ss[t].append(stats(t, j, X[:, t, c], d))
        rm = normed(xs, ss, lambda k: cst2[:, k:k + 1], PE.now())
        ready = [rm[k] for k in range(16)]
        fence()
        for h in range(0, 8, 4):
            bk = (M0, M1)[h // 4]
            for j in range(4):
                tk = tr(bk.t[:, j * P:(j + 1) * P], wsn[:, h + j, :], t_ws, bk.free, sig=(j == 3))
            e = act(wsT[:, h:h + 4, :], bk.t[:, :].rearrange("p (h q) -> p h q", h=4), ACT.Copy, tk)
            bk.free = [e]
        t_wsT = AC.now()

        for b in range(4):
            pr, t = stream(uh, ul, ready)
            for i in range(2):
                h = 2 * b + i
                p, y = pr[i].t, xc[:, h, :]
                wk = [cst2[:, 32 + 8 * k + h:33 + 8 * k + h] for k in range(4)]
                a = act(y, p[:, 0:T], ACT.Identity, t, scale=wk[2], bias=cst2[:, 64 + h:65 + h])
                d = stt(y[:, 1:T], p[:, 0:T - 1], wk[1], y[:, 1:T], M_, A_, a)
                d = stt(y[:, 2:T], p[:, 0:T - 2], wk[0], y[:, 2:T], M_, A_, d)
                d = stt(y[:, 0:T - 1], p[:, 1:T], wk[3], y[:, 0:T - 1], M_, A_, d)
                pr[i].free = [d]
        t_xc = DV.now()

        def lru(dr, hb):
            R, I, Aa, Th = lt
            yield from hold(M0)
            for q in range(4):
                h = hb + q
                wi = 8 * dr + h
                mm(M0.t[:, 0:T], lw[:, wi, :], xc[:, h, :], True, True, t_xc, t_lw1, t_lw2, M0.free)
                tk = mm(M0.t[:, T:2 * T], lw[:, 16 + wi, :], xc[:, h, :], True, True, sig=True)
                yield
                a = act(R[:, q, :], M0.t[:, 0:T], ACT.Sigmoid, tk, lru_free[0], bias=cst2[:, 80 + wi:81 + wi])
                b = act(I[:, q, :], M0.t[:, T:2 * T], ACT.Sigmoid, bias=cst2[:, 96 + wi:97 + wi])
                M0.free = [b]
            M0.held = False
            yield
            for q in range(4):
                wi = 8 * dr + hb + q
                e1 = act(Aa[:, q, :], R[:, q, :], ACT.Exp, AC.now(), scale=nsp[:, wi:wi + 1])
                e2 = act(Th[:, q, :], R[:, q, :], ACT.Tanh, scale=psp[:, wi:wi + 1])
            yield
            d = tt(R[:, :, :], Aa[:, :, :], Aa[:, :, :], M_, e1, e2)
            d = DV.do(lambda e: e.scalar_tensor_tensor(R[:, :, :], R[:, :, :], 1.0, Th[:, :, :], A_, M_), d)
            i1 = tt(I[:, :, :], I[:, :, :], xc[:, hb:hb + 4, :], M_, b)
            yield
            a = act(R[:, :, :], R[:, :, :], ACT.Sqrt, d)
            yield
            d = tt(R[:, :, :], R[:, :, :], I[:, :, :], M_, a, i1)
            for q in range(4):
                h = hb + q
                o = ho[:, h, :] if dr == 0 else Th[:, q, :]
                av, uv = Aa[:, q, :], R[:, q, :]
                if dr:
                    o, av, uv = o[:, ::-1], av[:, ::-1], uv[:, ::-1]
                f = DV.do(lambda e, o=o, av=av, uv=uv: e.tensor_tensor_scan(o, av, uv, 0.0, M_, A_), d)
            if dr:
                f = tt(ho[:, hb:hb + 4, :], ho[:, hb:hb + 4, :], Th[:, :, :], A_, f)
            lru_free[0] = [f]

        lru_free = [[]]
        tasks += [lru(dr, hb) for hb in (0, 4) for dr in (0, 1)]
        act_before = ACTIVE
        for b in range(4):
            pr, t = stream(uh, ul, ready, 0)
            for i in range(2):
                pr[i].free = [act(ggr[:, 2 * b + i, :], pr[i].t[:, 0:T], ACT.Gelu_apprx_tanh, t)]
            serial_step(tasks, 4)
        t_ggr = AC.now()
        vs = [[], []]
        for b in range(2):
            pr, t = stream(uh, ul, ready, 0)
            for i in range(2):
                v = vN[:, i, 512 * b:512 * (b + 1)]
                a = act(v, pr[i].t[:, :], ACT.Gelu_apprx_tanh, t)
                pr[i].free = [a]
                vs[i].append(stats(i, b, v, a))
            serial_step(tasks, 8)
        t_vn = []
        for i in range(2):
            a = finish_stats(i, 2, vs[i])
            s = act(sq[:, i:i + 1], mv[:, i, 1:2], ACT.Sqrt, a, bias=eps[:, 0:1])
            d = DV.do(lambda e, i=i: e.reciprocal(rstd[:, i:i + 1], sq[:, i:i + 1]), s)
            d = ts(vN[:, i, :], vN[:, i, :], mv[:, i, 0:1], rstd[:, i:i + 1], S_, M_, d)
            d = tt(vN[:, i, :], vN[:, i, :], lng[:, :], M_, d, t_lng)
            t_vn.append(tt(vN[:, i, :], vN[:, i, :], lnb[:, :], A_, d, t_lnb))
        for b in range(2):
            pr, t_u = stream(uh, ul, ready, 0)
            for i in range(2):
                pr[i].free = [act(uN[:, i, 512 * b:512 * (b + 1)], pr[i].t[:, :], ACT.Gelu_apprx_tanh, t_u)]
            serial_step(tasks, 8)
        t_un = AC.now()
        serial_step(tasks, 1000)
        d = tt(ho[:, :, :], ho[:, :, :], ggr[:, :, :], M_, t_ggr, lru_free[0])
        a = act(uh[:, 0:8, :], ho[:, :, :], ACT.Copy, d, t_u)
        d = tt(ul[:, 0:8, :], ho[:, :, :], uh[:, 0:8, :].bitcast(F32), S_, a, t_u)
        ready = [d] * 8
        gm = {}
        for i in range(2):
            for h0 in (0, 4):
                bk = (M0, M1)[h0 // 4]
                for q in range(4):
                    h = h0 + q
                    tk = mm(bk.t[:, q * P:(q + 1) * P], wsT[:, h, :], vN[:, i, h * P:(h + 1) * P], True, True,
                            t_wsT, t_vn[i], bk.free, sig=(q == 3))
                for q in range(4):
                    h = h0 + q
                    uu = uN[:, i, h * P:(h + 1) * P]
                    gm[i, h] = stt(uu, bk.t[:, q * P:(q + 1) * P], cst2[:, 72 + h:73 + h], uu, A_, M_, tk, t_un)
                bk.free = [gm[i, h0 + 3]]
        rm = to_uT(lambda t, k: uN[:, t, (k - 8) * P:(k - 7) * P], None, lambda t, k: gm[t, k - 8], t_u, ks=range(8, 16, 2))
        ready += [rm[k] for k in range(8, 16)]
        ss = residual(uh, ul, ready)

        fz = fence()
        area = Area(Z, END)
        xn = area.get("xn", [2, D])
        sc = area.get("sc", [2, 16, P])
        g2 = area.get("g2", [D])
        cand = area.get("cand", [8, 16, 16])
        oneh = area.get("oneh", [8, 16, 16])
        tsv = [area.get(f"tsv{i}", [16, 16]) for i in range(2)]
        tif = [area.get(f"tif{i}", [16, 16]) for i in range(2)]
        tiu = area.get("tiu", [16, 16], U32)
        bs = area.get("bs", [8, 16])
        pos = area.get("pos", [8, 16], U32)
        pi = area.get("pi", [8, 16], U32)
        pf = area.get("pf", [8, 16])
        sel = [area.get(f"sel{i}", [8, 16]) for i in range(2)]
        sg8 = area.get("sg8", [8])
        ids = [area.get(f"ids{i}", [128], U32) for i in range(2)]
        gw = [area.get(f"gw{i}", [8, 16]) for i in range(2)]
        dots = [area.get(f"dots{i}", [128]) for i in range(2)]
        Z3 = area.o
        qTt = area.get("qTt", [16, T])
        kyT = area.get("kyT", [16, P])
        kyN = at("kyN", [16, P], Z + 16384)
        t_g2 = load(AC, g2[:, :], io["ffn_norm_g_2"][0].partition_broadcast(P), "c_g2", fz)
        t_ky = load(PO, kyN[:, :, :], io["peer_sub_keys_2"][0].rearrange("h j n k -> n (h j) k"), "c_ky", fz)
        r = [rms(t, ss[t]) for t in range(2)]
        xo = {}
        for j in range(4):
            for t in range(2):
                c = slice(512 * j, 512 * (j + 1))
                xo[t, j] = stt(xn[:, t, c], X[:, t, c], rstd[:, t:t + 1], g2[:, c], M_, M_, r[t], t_g2)
        rm = to_uT(lambda t, k: xn[:, t, k * P:(k + 1) * P], None, lambda t, k: xo[t, k // 4], PE.now())
        ready = [rm[k] for k in range(16)]
        t_xn = DV.now()
        t_g2b = load(AC, g2[:, :], io["final_norm_g_2"].partition_broadcast(P), "c_fin", t_xn)
        for h in range(0, 16, 4):
            bk = (M0, M1)[(h // 4) % 2]
            for j in range(4):
                tk = tr(bk.t[:, j * P:(j + 1) * P], kyN[:, h + j, :], t_ky, bk.free, sig=(j == 3))
            e = act(kyT[:, h:h + 4, :], bk.t[:, :].rearrange("p (h q) -> p h q", h=4), ACT.Copy, tk)
            bk.free = [e]
        t_kyT = AC.now()
        for b in range(8):
            pr, t = stream(uh, ul, ready)
            for i in range(2):
                pr[i].free = [act(qTt[:, 2 * b + i, :], pr[i].t[:, 0:T], ACT.Copy, t)]
        t_q = AC.now()
        sc_t = {}
        for t in range(2):
            for h in range(0, 16, 4):
                bk = (M0, M1, T0, T1)[h // 4]
                for j in range(4):
                    tk = mm(bk.t[:, j * P:(j + 1) * P], qTt[:, h + j, t * P:(t + 1) * P], kyT[:, h + j, :], True, True,
                            t_q, t_kyT, bk.free, sig=(j == 3))
                e = act(sc[:, t, h:h + 4, :], bk.t[:, :].rearrange("p (h q) -> p h q", h=4), ACT.Copy, tk)
                bk.free = [e]
                sc_t[t, h // 4] = e
        LOWEST = -3.0e38

        def top16(vals, top, idx, *after):
            a = DV.do(lambda e: e.max(top[:, 0:8], vals), *after)
            b = DV.do(lambda e: e.max_index(idx[:, 0:8], top[:, 0:8], vals), a)
            c = DV.do(lambda e: e.match_replace(vals, top[:, 0:8], vals, LOWEST), a, b)
            d = DV.do(lambda e: e.max(top[:, 8:16], vals), c)
            return DV.do(lambda e: e.max_index(idx[:, 8:16], top[:, 8:16], vals), d)

        peer_t = {}

        def choose(t):
            for hp in range(16):
                d = top16(sc[:, t, hp, :], tsv[t][:, hp, :], tiu[:, hp, :], sc_t[t, hp // 4], DV.now())
                if hp % 2:
                    yield
            d = cp(tif[t][:, :, :], tiu[:, :, :], d)
            tv = tsv[t][:, :, :]
            rows_ = strided(tv, [32, 8], [1, 16], [0, 16])
            cols_ = strided(tsv[t][:, 1, :], [32, 8], [0, 16], [1, 16])
            d = tt(cand[:, :, :, :], rows_, cols_, A_, d)
            yield
            for h in range(8):
                d = top16(cand[:, h, :, :].rearrange("p a b -> p (a b)"), bs[:, h, :], pos[:, h, :], d)
                yield
            for side in range(2):
                if side == 0:
                    d = DV.do(lambda e: e.tensor_scalar(pi[:, :, :], pos[:, :, :], 4, None, ALU.logical_shift_right), d)
                else:
                    d = DV.do(lambda e: e.tensor_scalar(pi[:, :, :], pos[:, :, :], 15, None, ALU.bitwise_and), d)
                d = cp(pf[:, :, :], pi[:, :, :], d)
                ov = oneh[:, :, :, :].rearrange("p h w c -> p (h w) c")
                d = tt(ov, strided(pf[:, :, :], [1, 128], [0, 16]), strided(iota[:, :], [0, 128], [1, 16]), ALU.is_equal, d, t_io)
                yield
                tv = strided(tif[t][:, side, :], [32, 8], [0, 16], [1, 16])
                d = tt(oneh[:, :, :, :], oneh[:, :, :, :], tv, M_, d)
                yield
                d = DV.do(lambda e, side=side: e.tensor_reduce(sel[side][:, :, :].rearrange("p h w -> p (h w)"), ov, AX, A_), d)
                yield
            s0, s1 = (x[:, :, :].rearrange("p h w -> p (h w)") for x in sel)
            d = stt(s0, s0, 128.0, s1, M_, A_, d)
            peer_t["ids", t] = cp(ids[t][:, :], s0, d)
            gwv = gw[t][:, :, :]
            d = tt(gwv, bs[:, :, :], strided(bs[:, :, 0:1], [16, 8], [0, 16]), S_, d)
            a = act(gwv, gwv, ACT.Exp, d)
            d = DV.do(lambda e: e.tensor_reduce(sg8[:, :], gwv, AX, A_), a)
            d = DV.do(lambda e: e.reciprocal(sg8[:, :], sg8[:, :]), d)
            peer_t["gw", t] = tt(gwv, gwv, strided(sg8[:, :], [1, 8], [0, 16]), M_, d)

        for _ in choose(0):
            pass
        fz = fence()

        first_area = Area(u0, Z)
        rest_area = Area(Z3, END)

        def buffer(name):
            a = first_area if first_area.o + 8192 <= first_area.end else rest_area
            return a.get(name, [D])

        Ub = [buffer(f"Ub{i}") for i in range(NU)]
        Vb = [buffer(f"Vb{i}") for i in range(NV)]
        u_sem = [Counter(sem(f"us{i}")) for i in range(NU)]
        v_sem = [Counter(sem(f"vs{i}")) for i in range(NV)]
        eu, ev = io["peer_u_2"][0], io["peer_v_2"][0]
        u_in, v_in, dot_t, act_t, dg_t, v_use = {}, {}, {}, {}, {}, {}
        pend = [choose(1)]
        out_banks = [(M0, M1, T0, T1), (W0, W1, W2, W3)]
        out_sem = Counter(sem("outs"))
        out_d = out[0].rearrange("(t p) d -> p t d", p=P)

        def gather(buf, table, t, k, counter, *after):
            idx = ids[t][:, k:k + 1]
            return PO.dma(lambda e: e.indirect_dma_start(buf[:, :], None, table, bass.IndirectOffsetOnAxis(idx, 0)),
                          counter, *after)

        def get_u(n):
            t, k = divmod(n, 128)
            u_in[n] = gather(Ub[n % NU], eu, t, k, u_sem[n % NU], peer_t["ids", t], fz, dot_t.get(n - NU))

        def get_v(n):
            t, k = divmod(n, 128)
            v_in[n] = gather(Vb[n % NV], ev, t, k, v_sem[n % NV], peer_t["ids", t], fz, v_use.get(n - NV))

        def dot(n):
            t, k = divmod(n, 128)
            b = Ub[n % NU]
            dot_t[n] = DV.do(lambda e: e.tensor_tensor_reduce(b[:, :], b[:, :], xn[:, t, :], 1.0, 0.0, M_, A_, dots[t][:, k:k + 1]),
                             u_in[n], t_xn)
            if k % 16 == 15:
                h = k // 16
                c = slice(16 * h, 16 * h + 16)
                a = act(dots[t][:, c], dots[t][:, c], ACT.Gelu_apprx_tanh, dot_t[n])
                act_t[t, h] = tt(dots[t][:, c], dots[t][:, c], gw[t][:, h, :], M_, a, peer_t["gw", t])

        def accumulate(n):
            t, k = divmod(n, 128)
            dg_t[n] = act(diag[:, n % 4, :], ident[:, :], ACT.Copy, act_t[t, k // 16], v_use.get(n - 4), scale=dots[t][:, k:k + 1])
            for j in range(4):
                bk = out_banks[t][j]
                tk = mm(bk.t[:, :], diag[:, n % 4, :], Vb[n % NV][:, 512 * j:512 * (j + 1)], k == 0, k == 127,
                        dg_t[n], v_in[n], bk.free if k == 0 else None, sig=(j == 3))
            v_use[n] = tk

        def finish(t):
            tk = v_use[128 * t + 127]
            sx = []
            for j in range(4):
                c = slice(512 * j, 512 * (j + 1))
                d = tt(X[:, t, c], out_banks[t][j].t[:, :], X[:, t, c], A_, tk)
                sx.append(stats(t, j, X[:, t, c], d))
            r = rms(t, sx)
            for j in range(4):
                c = slice(512 * j, 512 * (j + 1))
                d = stt(X[:, t, c], X[:, t, c], rstd[:, t:t + 1], g2[:, c], M_, M_, r, t_g2b)
            SP.dma(lambda e: e.dma_start(out_d[:, t, :], X[:, t, :]), out_sem, d)

        for n in range(256 + VLAG):
            if n == 112:
                for _ in pend[0]:
                    pass
            if n < 256:
                get_u(n)
            if n >= VLAG:
                get_v(n - VLAG)
            if n < 256:
                dot(n)
            if n >= VLAG:
                accumulate(n - VLAG)
            if n < 112:
                for _ in range(1):
                    next(pend[0], None)
            if n == 127 + VLAG + 2:
                finish(0)
        finish(1)
        SP.wait((out_sem.sem, out_sem.n))

        blk = ctx.enter_context(nc.Block())
        blk.sync(SP.run)
        blk.tensor(PE.run)
        blk.scalar(AC.run)
        blk.vector(DV.run)
        blk.gpsimd(PO.run)


def serial_step(tasks, n):
    for _ in range(n):
        if not tasks:
            return
        try:
            next(tasks[0])
        except StopIteration:
            tasks.pop(0)


_INS = ['x', 'norm1_g', 'w_in', 'hg_lb_param', 'hg_norm_g', 'w_proj_a', 'w_proj_b', 'w_out', 'norm2_g', 'w_up',
        'conv_w', 'conv_b', 'w_down', 'norm_f_g', 'mix_norm_g_2', 'w_in_2', 'conv_w_2', 'conv_b_2', 'lru_w_a_2',
        'lru_b_a_2', 'lru_w_x_2', 'lru_b_x_2', 'lru_lambda_2', 'gmlp_ln_g_2', 'gmlp_ln_b_2', 'gmlp_w_s_2',
        'gmlp_b_s_2', 'w_out_2', 'ffn_norm_g_2', 'peer_w_q_2', 'peer_sub_keys_2', 'peer_u_2', 'peer_v_2',
        'final_norm_g_2']


def kernel(**inputs):
    import concourse.bacc as _bacc
    from concourse.bass_utils import run_bass_kernel_spmd as _run

    nc = _bacc.Bacc("TRN2", target_bir_lowering=False, num_devices=1)
    arrays, args = {}, {}
    for name in _INS:
        a = np.ascontiguousarray(inputs[name])
        arrays[f"in_{name}"] = a
        args[name] = nc.dram_tensor(f"in_{name}", a.shape, mybir.dt.from_np(a.dtype), kind="ExternalInput").ap()
    arrays["in_consts"] = shape_constants()
    args["consts"] = nc.dram_tensor("in_consts", (P, CONST_W), F32, kind="ExternalInput").ap()
    out = nc.dram_tensor("out_0", (1, T, D), F32, kind="ExternalOutput").ap()
    program(nc, args, out)
    r = _run(nc, [arrays], core_ids=[0])
    return r.results[0]["out_0"]
```

```python
import math
from contextlib import ExitStack

import numpy as np
import concourse.bass as bass
from concourse import mybir

F32 = mybir.dt.float32
F32R = mybir.dt.float32r
U32 = mybir.dt.uint32
ALU = mybir.AluOpType
ACT = mybir.ActivationFunctionType
AX = mybir.AxisListType.X

P = 128
T = 256
D = 2048
FF = 5632
EPS = 1e-6
NEG = -1e30
SCALE = 128.0 ** -0.5

NR = 3
NS = 4
LOOK = 3
NU = 4
NV = 11
VLAG = 8
GROUP = 4
VAHEAD = 1


class Lane:

    def __init__(self, sem):
        self.sem, self.n, self.ops, self.met = sem, 0, [], {}

    def wait(self, *after):
        for t in flat(after):
            sem, v = t
            if self.met.get(id(sem), 0) < v:
                self.met[id(sem)] = v
                self.ops.append(lambda e, sem=sem, v=v: e.wait_ge(sem, v))

    def do(self, fn, *after, sig=True):
        self.wait(*after)
        if not sig:
            self.ops.append(fn)
            return None
        self.n += 1
        self.ops.append(lambda e: fn(e).then_inc(self.sem, 1))
        return (self.sem, self.n)

    def dma(self, fn, counter, *after):
        self.wait(*after)
        counter.n += 16
        self.ops.append(lambda e: fn(e).then_inc(counter.sem, 16))
        return (counter.sem, counter.n)

    def now(self):
        return (self.sem, self.n) if self.n else None

    def run(self, e):
        for op in self.ops:
            op(e)


class Counter:
    def __init__(self, sem):
        self.sem, self.n = sem, 0


class Bank:
    def __init__(self, t):
        self.t, self.free, self.held = t, [], False


def flat(x):
    for y in x:
        if y is None:
            continue
        if isinstance(y, list):
            yield from flat(y)
        else:
            yield y


def strided(a, *dims):
    return bass.AP(tensor=a.tensor, offset=a.offset, ap=[list(a.ap[0])] + [list(d) for d in dims])


def cat(*parts):
    return list(parts)


CONST = {}
_o = 0
for _n, _w in (("ident", 128), ("cos", 256), ("sin", 256), ("amask", 1536), ("hmask", 1024), ("iota", 16)):
    CONST[_n] = (_o, _w)
    _o += _w
CONST_W = _o


def shape_constants():
    c = np.zeros((P, CONST_W), np.float32)

    def put(name, v):
        o, w = CONST[name]
        c[:, o:o + w] = v.reshape(P, w)

    put("ident", np.eye(P, dtype=np.float32))
    half = 64
    inv = np.exp(np.float32(-math.log(10000.0)) * np.arange(half, dtype=np.float32) * np.float32(2.0 / 128))
    ang = np.arange(T, dtype=np.float32)[:, None] * inv.astype(np.float32)[None, :]
    co, si = np.cos(ang).astype(np.float32), np.sin(ang).astype(np.float32)
    put("cos", np.concatenate([co, co], 1).reshape(2, P, 128).transpose(1, 0, 2))
    put("sin", np.concatenate([-si, si], 1).reshape(2, P, 128).transpose(1, 0, 2))
    t, s = np.arange(T)[:, None], np.arange(T)[None, :]
    m = np.zeros((3, T, T), np.float32)
    for g, dil in enumerate((1, 4, 16)):
        ok = (t >= s) & ((t - s) % dil == 0) & (t - s <= 128 * dil)
        m[g] = np.where(ok, 0.0, NEG)
    put("amask", m.reshape(3, 2, P, T).transpose(2, 1, 0, 3))
    s, t = np.arange(P)[:, None], np.arange(P)[None, :]
    h = np.zeros((P, 8, P), np.float32)
    for lv in range(7):
        w = 1 << lv
        h[:, lv] = (s // (2 * w) == t // (2 * w)) & (s % (2 * w) < w) & (t % (2 * w) >= w)
    h[:, 7] = s == t
    put("hmask", h)
    put("iota", np.tile(np.arange(16, dtype=np.float32), (P, 1)))
    return c


def program(nc, io, out):
    with ExitStack() as ctx:
        def sem(name):
            return ctx.enter_context(nc.semaphore(name))

        SP, PE, AC, DV, PO = (Lane(sem(f"lane_{n}")) for n in ("sp", "pe", "act", "dve", "pool"))

        BASE = 16512
        top = [BASE]

        def at(name, shape, offset, dt=F32):
            return nc.alloc_sbuf_tensor_at(name, [P] + list(shape), dt, offset=offset)

        def low(name, shape, dt=F32):
            n = int(np.prod(shape)) * 4
            t = at(name, shape, top[0], dt)
            top[0] += (n + 31) // 32 * 32
            return t

        class Area:
            def __init__(self, start, end):
                self.o, self.end = start, end

            def get(self, name, shape, dt=F32):
                t = at(name, shape, self.o, dt)
                self.o += (int(np.prod(shape)) * 4 + 31) // 32 * 32
                assert self.o <= self.end, (name, self.o, self.end)
                return t

        ident = low("ident", [128])
        cst1 = low("cst1", [64])
        cst2 = low("cst2", [128])
        cw = low("cw", [4, 88])
        iota = low("iota", [16])
        ones = low("ones", [256])
        hgn = low("hgn", [128])
        eps = low("eps", [1])
        lb = low("lb", [16])
        oml = low("oml", [16])
        st6 = low("st6", [2, 4, 6])
        mv = low("mv", [2, 2])
        ms = low("ms", [2])
        sq = low("sq", [2])
        rstd = low("rstd", [2])
        nsp = low("nsp", [16])
        psp = low("psp", [16])
        diag = low("diag", [4, 128])
        X = low("X", [2, D])
        u0 = top[0]
        uh = low("uh", [16, T], F32R)
        ul = low("ul", [16, T], F32R)
        raw = low("raw", [NR, 2048])
        wh = low("wh", [NS, 1024], F32R)
        wl = low("wl", [NS, 1024], F32R)
        Z = top[0]
        END = 229344
        bank_names = ["W0", "W1", "W2", "W3", "T0", "T1", "M0", "M1"]
        W0, W1, W2, W3, T0, T1, M0, M1 = (
            Bank(ctx.enter_context(nc.psum_tensor(n, [P, 512], F32))) for n in bank_names)
        pairs = [(W0, W1), (W2, W3)]

        def act(o, i, f, *after, **kw):
            return AC.do(lambda e: e.activation(o, i, f, **kw), *after)

        def tt(o, a, b, op, *after, lane=None):
            return (lane or DV).do(lambda e: e.tensor_tensor(o, a, b, op), *after)

        def ts(o, a, s1, s2, op0, op1, *after, lane=None):
            if op1 is None:
                return (lane or DV).do(lambda e: e.tensor_scalar(o, a, s1, None, op0), *after)
            return (lane or DV).do(lambda e: e.tensor_scalar(o, a, s1, s2, op0, op1), *after)

        def stt(o, a, s, b, op0, op1, *after):
            return DV.do(lambda e: e.scalar_tensor_tensor(o, a, s, b, op0, op1), *after)

        def cp(o, i, *after):
            return DV.do(lambda e: e.tensor_copy(o, i), *after)

        def mm(o, l, r, start, stop, *after, sig=False):
            return PE.do(lambda e: e.matmul(o, l, r, start=start, stop=stop), *after, sig=sig)

        def tr(o, i, *after, sig=False, n=P):
            return PE.do(lambda e: e.transpose(o, i, ident[0:n, 0:n]), *after, sig=sig)

        def load(lane, o, i, name, *after):
            return lane.dma(lambda e: e.dma_start(o, i), Counter(sem(name)), *after)

        def fence():
            t = [PE.now(), AC.now(), DV.now(), PO.now()]
            for lane in (AC, DV, PO):
                lane.wait(t)
            return t

        A_, S_, M_ = ALU.add, ALU.subtract, ALU.mult

        def wide(w, c0, kt):
            return dict(kind="n", kt=kt, kc=4, n=512,
                        src=w[:, c0:c0 + 512].rearrange("(k p) n -> p k n", p=P))

        def tall(w, c0, kt):
            return dict(kind="s", kt=kt, kc=8, n=256,
                        src=w[:, c0:c0 + 256].rearrange("(k p) n -> p k n", p=P))

        w_in, w_pa, w_pb, w_out = io["w_in"][0], io["w_proj_a"][0], io["w_proj_b"][0], io["w_out"][0]
        w_up, w_down = io["w_up"][0], io["w_down"][0]
        w_in2, w_out2, w_q = io["w_in_2"][0], io["w_out_2"][0], io["peer_w_q_2"][0]
        blocks = []
        for base in (11264, 9728, 8192):
            blocks += [wide(w_in, base + 512 * g, 16) for g in range(3)]
        ORDER = [("G", 0), ("G", 1), ("B", 0), ("G", 2), ("B", 1), ("G", 3), ("B", 2), ("B", 3)]
        for what, g in ORDER:
            if what == "G":
                blocks += [wide(w_in, 4096 + 512 * g, 16), wide(w_in, 6144 + 512 * g, 16)]
                blocks += [tall(w_in, b + 512 * g + 256 * i, 16) for i in range(2) for b in (0, 2048)]
            else:
                blocks += [wide(w_in, 14848 + 512 * g, 16), wide(w_pb, 512 * g, 4)]
        for b in blocks[9:]:
            b["shared"] = True
        for n in range(4):
            blocks += [wide(w_in, 12800 + 512 * n, 16), wide(w_pa, 512 * n, 16)]
        blocks += [wide(w_out, 512 * n, 16) for n in range(4)]
        for j in range(22):
            blocks += [tall(w_up, 256 * j, 16), tall(w_up, FF + 256 * j, 16)]
        blocks += [wide(w_down, 512 * n, 44) for n in range(4)]
        blocks += [tall(w_in2, 256 * j, 16) for j in range(4)]
        blocks += [wide(w_in2, c, 16) for c in (3072, 3584, 2048, 2560)]
        blocks += [tall(w_in2, 256 * j, 16) for j in range(4, 8)]
        blocks += [wide(w_out2, 512 * n, 16) for n in range(4)]
        blocks += [dict(tall(w_q, 256 * j, 16), shared=True) for j in range(8)]

        chunks, subs = [], []
        for b in blocks:
            b["first"] = len(subs)
            for c in range(b["kt"] // b["kc"]):
                chunks.append((b, c * b["kc"]))
                for half in range(2):
                    subs.append((b, c * b["kc"] + half * (b["kc"] // 2), len(chunks) - 1, half))
        raw_sems = [Counter(sem(f"raw{i}")) for i in range(NR)]
        landed, split, used = {}, {}, {}

        def fetch(c):
            b, k0 = chunks[c]
            dst = raw[:, c % NR, :].rearrange("p (k n) -> p k n", n=b["n"])
            src = b["src"][:, k0:k0 + b["kc"], :]
            after = [split[2 * (c - NR)], split[2 * (c - NR) + 1]] if c >= NR else None
            landed[c] = SP.dma(lambda e: e.dma_start(dst, src), raw_sems[c % NR], after)

        conv_at = [0]

        def convert_upto(s_end):
            while conv_at[0] < min(s_end, len(subs)):
                s = conv_at[0]
                _, _, c, half = subs[s]
                r = raw[:, c % NR, half * 1024:(half + 1) * 1024]
                ta = act(wh[:, s % NS, :], r, ACT.Copy, landed[c], used.get(s - NS))
                lane = PO if subs[s][0].get("shared") and s % 2 else DV
                split[s] = tt(wl[:, s % NS, :], r, wh[:, s % NS, :].bitcast(F32), S_, ta, used.get(s - NS), lane=lane)
                if half == 1 and c + NR < len(chunks):
                    fetch(c + NR)
                conv_at[0] += 1

        tasks = []
        pace = dict(active=2, credit=0.0)

        def step():
            if tasks:
                g = tasks.pop(0)
                try:
                    cost = next(g)
                    tasks.insert(min(pace["active"] - 1, len(tasks)), g)
                    return cost
                except StopIteration:
                    return 0.5
            return 0.0

        def drain():
            while tasks:
                step()

        block_at = [0]

        def stream(xh, xl, ready, steps=1):
            b = blocks[block_at[0]]
            pr = pairs[block_at[0] % 2]
            block_at[0] += 1
            n_sub = 2 * (b["kt"] // b["kc"])
            for i in range(n_sub):
                s = b["first"] + i
                convert_upto(s + 1 + LOOK)
                _, k0, _, _ = subs[s]
                kc = b["kc"] // 2
                H = wh[:, s % NS, :].rearrange("p (k n) -> p k n", n=b["n"])
                L = wl[:, s % NS, :].rearrange("p (k n) -> p k n", n=b["n"])
                PE.wait(split[s])
                if i == 0:
                    PE.wait(pr[0].free, pr[1].free)
                for k in range(kc):
                    kk = k0 + k
                    PE.wait(ready[kk])
                    first, last = kk == 0, kk == b["kt"] - 1
                    for h in range(2):
                        end = k == kc - 1 and h == 1
                        if b["kind"] == "n":
                            o = pr[h].t[:, :]
                            th, tl = xh[:, kk, h * P:(h + 1) * P], xl[:, kk, h * P:(h + 1) * P]
                            mm(o, th, H[:, k, :], first, False)
                            mm(o, th, L[:, k, :], False, False)
                            t = mm(o, tl, H[:, k, :], False, last, sig=end)
                        else:
                            o = pr[h].t[:, 0:T]
                            vh, vl = H[:, k, h * P:(h + 1) * P], L[:, k, h * P:(h + 1) * P]
                            mm(o, vh, xh[:, kk, :], first, False)
                            mm(o, vh, xl[:, kk, :], False, False)
                            t = mm(o, vl, xh[:, kk, :], False, last, sig=end)
                used[s] = t
                pace["credit"] = min(pace["credit"], 0.0) + steps
                while tasks and pace["credit"] > 0:
                    pace["credit"] -= step()
            return pr, t

        def hold(*bs):
            while any(b.held for b in bs):
                yield 0.3
            for b in bs:
                b.held = True

        def stats(t, j, src, *after):
            return DV.do(lambda e: e.bn_stats(st6[:, t, j, :], src), *after)

        def finish_stats(t, n, *after):
            a = DV.do(lambda e: e.bn_aggr(mv[:, t, :], st6[:, t, 0:n, :].rearrange("p a b -> p (a b)")), *after)
            return a

        def rms(t, *after):
            a = finish_stats(t, 4, *after)
            m = stt(ms[:, t:t + 1], mv[:, t, 0:1], mv[:, t, 0:1], mv[:, t, 1:2], M_, A_, a)
            s = act(sq[:, t:t + 1], ms[:, t:t + 1], ACT.Sqrt, m, bias=eps[:, 0:1])
            return DV.do(lambda e: e.reciprocal(rstd[:, t:t + 1], sq[:, t:t + 1]), s)

        def to_uT(piece, gcol, ready_in, after_pe, ks=range(0, 16, 2)):
            ready = {}
            for k in ks:
                bk = (T0, T1, M0, M1)[(k // 2) % 4]
                for kk in (k, k + 1):
                    for t in range(2):
                        o = bk.t[:, (kk - k) * T + t * P:(kk - k) * T + (t + 1) * P]
                        tk = tr(o, piece(t, kk), ready_in(t, kk), bk.free, sig=(kk == k + 1 and t == 1))
                if gcol is None:
                    a = act(uh[:, k:k + 2, :], bk.t[:, :].rearrange("p (k t) -> p k t", k=2), ACT.Copy, tk, after_pe)
                    d = tt(ul[:, k:k + 2, :], bk.t[:, :].rearrange("p (k t) -> p k t", k=2),
                           uh[:, k:k + 2, :].bitcast(F32), S_, a, after_pe)
                    ready[k] = ready[k + 1] = d
                else:
                    for kk in (k, k + 1):
                        v = bk.t[:, (kk - k) * T:(kk - k + 1) * T]
                        a = act(uh[:, kk, :], v, ACT.Copy, tk, after_pe, scale=gcol(kk))
                    for kk in (k, k + 1):
                        v = bk.t[:, (kk - k) * T:(kk - k + 1) * T]
                        d = stt(ul[:, kk, :], v, gcol(kk), uh[:, kk, :].bitcast(F32), M_, S_, a, after_pe)
                        ready[kk] = d
                bk.free = [a, d]
            return ready

        def scaled(xs, src_after):
            r = [rms(t, src_after[t]) for t in range(2)]
            out = {}
            for j in range(4):
                c = slice(512 * j, 512 * (j + 1))
                out[0, j] = act(xs[:, 0, c], X[:, 0, c], ACT.Copy, r[0], scale=rstd[:, 0:1])
                out[1, j] = ts(xs[:, 1, c], X[:, 1, c], rstd[:, 1:2], None, M_, None, r[1])
            return out

        def normed(xs, src_after, gcol, after_pe):
            ok = scaled(xs, src_after)
            return to_uT(lambda t, k: xs[:, t, k * P:(k + 1) * P], gcol, lambda t, k: ok[t, k // 4], after_pe)

        con = io["consts"]

        def cslice(n):
            o, w = CONST[n]
            return con[:, o:o + w]

        x_dram = io["x"][0].rearrange("(t p) d -> p t d", p=P)
        t_id = load(AC, ident[:, :], cslice("ident"), "c_id")
        tx = [load(SP, X[:, t, :], x_dram[:, t, :], f"x{t}") for t in range(2)]
        st_area = Area(Z, END)
        xs = st_area.get("xs_a", [2, D])
        st1 = st_area.get("st1", [128])
        st2 = st_area.get("st2", [128])
        cws = st_area.get("cws", [4, 128])
        lbt = st_area.get("lbt", [16])
        c1 = Counter(sem("c_st1"))
        c2 = Counter(sem("c_st2"))
        c3 = Counter(sem("c_cw"))

        def rows(dst, r0, src, counter):
            n = src.shape[0]
            return AC.dma(lambda e: e.dma_start(dst[r0:r0 + n, :], src), counter)

        rows(st1, 0, io["norm1_g"].rearrange("o (k p) -> (o k) p", p=P), c1)
        rows(st1, 16, io["norm2_g"].rearrange("o (k p) -> (o k) p", p=P), c1)
        t_st1 = rows(st1, 32, io["hg_lb_param"].rearrange("o (k p) -> (o k) p", p=P), c1)
        for r0, nm in ((0, "mix_norm_g_2"), (16, "ffn_norm_g_2"), (80, None)):
            if nm:
                rows(st2, r0, io[nm].rearrange("o (k p) -> (o k) p", p=P), c2)
        rows(st2, 32, io["conv_w_2"][0].rearrange("o (k p) -> (o k) p", p=P), c2)
        rows(st2, 64, io["conv_b_2"].rearrange("o (k p) -> (o k) p", p=P), c2)
        rows(st2, 72, io["gmlp_b_s_2"][0], c2)
        rows(st2, 80, io["lru_b_a_2"][0].rearrange("o (k p) -> (o k) p", p=P), c2)
        rows(st2, 96, io["lru_b_x_2"][0].rearrange("o (k p) -> (o k) p", p=P), c2)
        t_st2 = rows(st2, 112, io["lru_lambda_2"][0].rearrange("o (k p) -> (o k) p", p=P), c2)
        AC.dma(lambda e: e.dma_start(cws[0:88, 0:3, :], io["conv_w"][0].rearrange("o (k p) -> k o p", p=P)), c3)
        t_cw = AC.dma(lambda e: e.dma_start(cws[0:88, 3, :], io["conv_b"][0].rearrange("(k p) -> k p", p=P)), c3)
        t_hgn = load(AC, hgn[:, :], io["hg_norm_g"][0].partition_broadcast(P), "c_hgn")
        t_io = load(AC, iota[:, :], cslice("iota"), "c_iota")
        t_ones = PO.do(lambda e: e.memset(ones[:, :], 1.0))
        t_eps = PO.do(lambda e: e.memset(eps[:, :], EPS))
        AC.wait(t_eps)
        for c in range(NR):
            fetch(c)
        ss = [[stats(t, j, X[:, t, 512 * j:512 * (j + 1)], tx[t]) for j in range(4)] for t in range(2)]
        k1 = tr(W0.t[:, 0:64], st1[0:64, :], t_st1, t_id, n=64, sig=True)
        q1 = cp(cst1[:, :], W0.t[:, 0:64], k1)
        AC.wait(q1)
        DV.wait(q1)
        W0.free = [q1]
        ready = normed(xs, ss, lambda k: cst1[:, k:k + 1], None)
        ready = [ready[k] for k in range(16)]
        convert_upto(LOOK)

        k2 = tr(W2.t[:, 64:192], st2[:, :], t_st2, sig=True)
        for o in range(4):
            k3 = tr(W3.t[:, 88 * o:88 * o + 88], cws[0:88, o, :], t_cw, sig=(o == 3), n=88)
        q2 = cp(cst2[:, :], W2.t[:, 64:192], k2)
        q3 = cp(cw[:, :, :], W3.t[:, 0:352].rearrange("p (o k) -> p o k", o=4), k3)
        W2.free, W3.free = [q2], [q3]
        AC.wait(q2, q3)
        l1 = tt(lbt[:, :], cst1[:, 32:48], cst1[:, 48:64], S_, q1)
        t_lb = [act(lb[:, :], lbt[:, :], ACT.Sigmoid, l1), act(oml[:, :], lbt[:, :], ACT.Sigmoid, l1, scale=-1.0)]
        DV.wait(t_lb, q1, q2, q3)
        lam = cst2[:, 112:128]
        sa = [st_area.get(f"sp{i}", [16]) for i in range(5)]
        z = ts(sa[0][:, :], lam, -1.0, None, M_, None)
        z = tt(sa[0][:, :], lam, sa[0][:, :], ALU.min, z)
        z = act(sa[1][:, :], sa[0][:, :], ACT.Exp, z)
        z = ts(sa[2][:, :], sa[1][:, :], 2.0, None, A_, None, z)
        z = DV.do(lambda e: e.reciprocal(sa[3][:, :], sa[2][:, :]), z)
        z = tt(sa[2][:, :], sa[1][:, :], sa[3][:, :], M_, z)
        z = tt(sa[3][:, :], sa[2][:, :], sa[2][:, :], M_, z)
        z = ts(sa[4][:, :], sa[3][:, :], 2.0 / 17, 2.0 / 15, M_, A_, z)
        for c in (13, 11, 9, 7, 5, 3, 1):
            z = tt(sa[4][:, :], sa[4][:, :], sa[3][:, :], M_, z)
            z = ts(sa[4][:, :], sa[4][:, :], 2.0 / c, None, A_, None, z)
        z = tt(sa[4][:, :], sa[4][:, :], sa[2][:, :], M_, z)
        z1 = ts(sa[0][:, :], lam, -1.0, 0.0, M_, ALU.max, z)
        z = tt(sa[4][:, :], sa[4][:, :], sa[0][:, :], A_, z, z1)
        ts(nsp[:, :], sa[4][:, :], -8.0, None, M_, None, z)
        t_nsp = ts(psp[:, :], sa[4][:, :], 8.0, None, M_, None, z)
        AC.wait(t_nsp)


        area = Area(Z, END)
        obh = area.get("obh", [4, T], F32R)
        obl = area.get("obl", [4, T], F32R)
        qb = area.get("qb", [4, T])
        kb = area.get("kb", [4, T])
        Gb = area.get("Gb", [4, T])
        vb = [area.get(f"vb{i}", [2, 512]) for i in range(2)]
        gb = [area.get(f"gb{i}", [2, 512]) for i in range(2)]
        Z2 = area.o
        fz = fence()
        area = Area(Z2, END)
        qT = area.get("qT", [12, T])
        kT = area.get("kT", [12, T])
        vA = area.get("vA", [2, 1536])
        Sb = [area.get(f"S{i}", [768]) for i in range(2)]
        pT = area.get("pT", [6, P])
        r1 = area.get("r1", [512])
        r2 = [area.get(f"r2{i}", [512]) for i in range(2)]
        cos = area.get("cosT", [2, 128])
        sin = area.get("sinT", [2, 128])
        amask = area.get("amask", [2, 3, T])
        sm = area.get("sm", [8, 4])
        t_cos = load(PO, cos[:, :, :], cslice("cos").rearrange("p (t d) -> p t d", t=2), "c_cos", fz)
        t_sin = load(PO, sin[:, :, :], cslice("sin").rearrange("p (t d) -> p t d", t=2), "c_sin", fz)
        t_am = load(PO, amask[:, :, :, :], cslice("amask").rearrange("p (t g s) -> p t g s", t=2, g=3), "c_am", fz)

        for g in range(3):
            pr, t = stream(uh, ul, ready)
            for i in range(2):
                pr[i].free = [act(vA[:, i, 512 * g:512 * (g + 1)], pr[i].t[:, :], ACT.Copy, t)]
        t_v = AC.now()
        r2_free = [[], []]
        rope_t = []
        for dst in (kT, qT):
            for g in range(3):
                pr, t = stream(uh, ul, ready)
                for i in range(2):
                    pv = pr[i].t[:, :].rearrange("p (h d) -> p h d", h=4)
                    v1 = r1[:, :].rearrange("p (h d) -> p h d", h=4)
                    v2 = r2[i][:, :].rearrange("p (h d) -> p h d", h=4)
                    a = tt(v1, pv, strided(cos[:, i, :], [0, 4], [1, 128]), M_, t, t_cos, DV.now())
                    b = tt(v2[:, :, 0:64], pv[:, :, 64:128], strided(sin[:, i, 0:64], [0, 4], [1, 64]), M_, t_sin, r2_free[i])
                    c = tt(v2[:, :, 64:128], pv[:, :, 0:64], strided(sin[:, i, 64:128], [0, 4], [1, 64]), M_)
                    pr[i].free = [c]
                    d = tt(r2[i][:, :], r1[:, :], r2[i][:, :], A_, a, b, c)
                    bk = (T0, T1)[i]
                    for h in range(4):
                        tk = tr(bk.t[:, h * P:(h + 1) * P], r2[i][:, h * P:(h + 1) * P], d, bk.free, sig=(h == 3))
                    r2_free[i] = [tk]
                    e = act(dst[:, 4 * g:4 * g + 4, i * P:(i + 1) * P],
                            bk.t[:, :].rearrange("p (h t) -> p h t", h=4), ACT.Copy, tk)
                    bk.free = [e]
                    rope_t = [e]

        s_free, p_free, ob_t = [[], []], [[]], []

        def attend(n, hg, t):
            ns = 1 + t
            w = P * ns
            S = Sb[n % 2]
            sv = S[:, 0:3 * w].rearrange("p (g s) -> p g s", g=3)
            yield from hold(M0, M1)
            for g in range(3):
                o = M0.t[:, g * w:(g + 1) * w] if (t == 0 or g < 2) else M1.t[:, 0:w]
                tk = mm(o, qT[:, 4 * g + hg, t * P:(t + 1) * P], kT[:, 4 * g + hg, 0:w], True, True,
                        rope_t, t_v, M0.free, M1.free, sig=(g == 2))
            yield 0.5
            if t == 0:
                d = tt(sv, M0.t[:, 0:3 * w].rearrange("p (g s) -> p g s", g=3), amask[:, 0, :, 0:w], A_, tk, t_am, s_free[n % 2])
                dd = [d]
            else:
                d1 = tt(sv[:, 0:2, :], M0.t[:, :].rearrange("p (g s) -> p g s", g=2), amask[:, 1, 0:2, :], A_, tk, t_am, s_free[n % 2])
                d2 = tt(sv[:, 2, :], M1.t[:, 0:w], amask[:, 1, 2, :], A_)
                dd = [d1, d2]
            M0.free = M1.free = dd
            M0.held = M1.held = False
            m = DV.do(lambda e: e.tensor_reduce(sm[:, n, 0:1], S[:, 0:3 * w], AX, ALU.max), dd)
            m = ts(sm[:, n, 1:2], sm[:, n, 0:1], -SCALE, None, M_, None, m)
            yield 2.2
            a = act(S[:, 0:3 * w], S[:, 0:3 * w], ACT.Exp, m, dd, scale=SCALE, bias=sm[:, n, 1:2], accum_out=sm[:, n, 2:3])
            yield 0.5
            r = DV.do(lambda e: e.reciprocal(sm[:, n, 3:4], sm[:, n, 2:3]), a)
            r = ts(S[:, 0:3 * w], S[:, 0:3 * w], sm[:, n, 3:4], None, M_, None, r)
            yield from hold(T0, T1)
            nb = 3 * ns
            for j in range(nb):
                bk, c = (T0, j) if j < 4 else (T1, j - 4)
                tk = tr(bk.t[:, c * P:(c + 1) * P], S[:, j * P:(j + 1) * P], r, bk.free, sig=(j == nb - 1))
            s_free[n % 2] = [tk]
            yield 1.0
            n0 = min(nb, 4)
            e1 = act(pT[:, 0:n0, :], T0.t[:, 0:n0 * P].rearrange("p (j t) -> p j t", t=P), ACT.Copy, tk, p_free[0])
            e2 = cp(pT[:, 4:6, :], T1.t[:, 0:2 * P].rearrange("p (j t) -> p j t", t=P), tk, p_free[0]) if nb > 4 else None
            T0.free, T0.held = [e1], False
            yield 0.5
            o = T1.t[:, 256:384]
            for j in range(nb):
                g, si = j // ns, j % ns
                tk = mm(o, vA[:, si, (4 * g + hg) * P:(4 * g + hg + 1) * P], pT[:, j, :], j == 0, j == nb - 1,
                        e1, e2, T1.free, sig=(j == nb - 1))
            p_free[0] = [tk]
            yield 0.7
            a = act(obh[:, hg, t * P:(t + 1) * P], o, ACT.Copy, tk)
            d = tt(obl[:, hg, t * P:(t + 1) * P], o, obh[:, hg, t * P:(t + 1) * P].bitcast(F32), S_, a)
            T1.free, T1.held = [e2, a, d], False
            ob_t[:] = [d]

        for n in range(8):
            tasks.append(attend(n, n // 2, n % 2))

        hg_mem = {}

        def hg_setup():
            drain()
            fz = fence()
            area = Area(Z2, END)
            hg_mem["oah"] = area.get("oah", [16, T], F32R)
            hg_mem["oal"] = area.get("oal", [16, T], F32R)
            hg_mem["E"] = [area.get(f"E{i}", [8, T]) for i in range(2)]
            hg_mem["prod"] = area.get("prod", [8, P])
            hg_mem["mask"] = area.get("hmask", [8, P])
            hg_mem["AT"] = [area.get(f"AT{i}", [3, P]) for i in range(2)]
            hg_mem["o"] = area.get("o_n", [2, P])
            hg_mem["junk"] = area.get("junk", [P])
            hg_mem["s"] = area.get("hs", [2, 2, 4])
            hg_mem["t_mask"] = load(PO, hg_mem["mask"][:, :, :], cslice("hmask").rearrange("p (l t) -> p l t", l=8), "c_hm", fz)

        E_free, AT_free, o_free, prod_free = [[], []], [[], []], [[]], [[]]
        grp_done = [[], []]
        left = [2] * 8

        def finish_pair(p):
            while p >= 0 and left[p]:
                step()

        vg_done = [[], []]

        def halves(E, lv):
            w = 1 << lv
            v = E[:, lv, :].rearrange("p (b c) -> p b c", c=2 * w)
            return v[:, :, 0:w], v[:, :, w:2 * w]

        def scan_head(g, j, t_lnf):
            hd, pair, jv = 4 * g + j, 2 * g + j // 2, j
            j = j % 2 + 2 * (pair % 2)
            E, AT = hg_mem["E"][j % 2], hg_mem["AT"][j % 2]
            prod, mask, on, junk, hs = (hg_mem[k] for k in ("prod", "mask", "o", "junk", "s"))
            oah, oal = hg_mem["oah"], hg_mem["oal"]
            G = Gb[:, j, :]
            c = DV.do(lambda e: e.tensor_tensor_scan(G, ones[:, :], G, 0.0, M_, A_), t_lnf, t_ones)
            for lv in range(8):
                w = 1 << lv
                gv = G.rearrange("p (b c) -> p b c", c=2 * w)
                ref = strided(G[:, w - 1:w], [2 * w, T // (2 * w)], [0, w])
                el, er = halves(E, lv)
                d1 = tt(el, ref, gv[:, :, 0:w], S_, c, E_free[j % 2])
                d2 = tt(er, gv[:, :, w:2 * w], ref, S_)
                if lv in (1, 3, 5):
                    yield 1.0
            yield 1.0
            a1 = act(E[:, 0:4, :], E[:, 0:4, :], ACT.Exp, d2)
            a2 = act(E[:, 4:8, :], E[:, 4:8, :], ACT.Exp, d2)
            yield 1.0
            for lv in range(8):
                w = 1 << lv
                el, er = halves(E, lv)
                kv = kb[:, j, :].rearrange("p (b c) -> p b c", c=2 * w)
                qv = qb[:, j, :].rearrange("p (b c) -> p b c", c=2 * w)
                m1 = tt(el, el, kv[:, :, 0:w], M_, a1 if lv < 4 else a2)
                m2 = tt(er, er, qv[:, :, w:2 * w], M_)
                if lv in (1, 3, 5, 7):
                    yield 0.9
            for i in range(2):
                cs = slice(i * P, (i + 1) * P)
                yield from hold(M0, M1)
                for lv in range(8):
                    bk = M0 if lv < 4 else M1
                    o = bk.t[:, (lv % 4) * P:(lv % 4 + 1) * P]
                    if lv < 7:
                        tk = mm(o, E[:, lv, cs], E[:, lv, cs], True, True, m2, bk.free)
                    else:
                        tk = mm(o, kb[:, j, cs], qb[:, j, cs], True, True, sig=True)
                yield 0.8
                p1 = tt(prod[:, 0:4, :], M0.t[:, :].rearrange("p (l t) -> p l t", l=4), mask[:, 0:4, :], M_, tk, hg_mem["t_mask"], prod_free[0])
                p2 = tt(prod[:, 4:8, :], M1.t[:, :].rearrange("p (l t) -> p l t", l=4), mask[:, 4:8, :], M_)
                M0.free, M1.free = [p1], [p2]
                M0.held = M1.held = False
                s = DV.do(lambda e, i=i: e.tensor_reduce(AT[:, 2 * i, :], prod[:, :, :].rearrange("p l t -> p t l"), AX, A_), p1, p2, AT_free[j % 2])
                prod_free[0] = [s]
                yield 2.4
            yield from hold(T0)
            tk = mm(T0.t[:, 0:P], E[:, 7, 0:P], E[:, 7, P:T], True, True, T0.free, sig=True)
            E_free[j % 2] = [tk]
            yield 0.7
            a = act(AT[:, 1, :], T0.t[:, 0:P], ACT.Copy, tk, AT_free[j % 2])
            yield 0.7
            v0, v1 = vb[g % 2][:, 0, jv * P:(jv + 1) * P], vb[g % 2][:, 1, jv * P:(jv + 1) * P]
            mm(T0.t[:, P:2 * P], AT[:, 0, :], v0, True, True, s, a)
            mm(T0.t[:, 2 * P:3 * P], AT[:, 1, :], v0, True, False)
            tk = mm(T0.t[:, 2 * P:3 * P], AT[:, 2, :], v1, False, True, sig=True)
            AT_free[j % 2] = [tk]
            yield 0.7
            h2 = hs[:, j % 2, :, :]
            for i in range(2):
                a = act(junk[:, :], T0.t[:, (1 + i) * P:(2 + i) * P], ACT.Square, tk, AC.now(), accum_out=h2[:, i, 0:1])
            x_, y_, w_ = h2[:, :, 0], h2[:, :, 1], h2[:, :, 2]
            d = ts(x_, x_, 1.0 / P, EPS, M_, A_, a)
            a = act(y_, x_, ACT.Ln, d)
            a = act(y_, y_, ACT.Exp, a, scale=-0.5)
            yield 0.7
            d = tt(w_, y_, y_, M_, a)
            d = tt(w_, w_, x_, M_, d)
            d = ts(w_, w_, -0.5, 1.5, M_, A_, d)
            d = tt(y_, y_, w_, M_, d)
            for i in range(2):
                e = stt(on[:, i, :], T0.t[:, (1 + i) * P:(2 + i) * P], h2[:, i, 1:2], gb[g % 2][:, i, jv * P:(jv + 1) * P],
                        M_, M_, d, o_free[0])
            T0.free, T0.held = [e], False
            yield from hold(T1)
            for i in range(2):
                tk = tr(T1.t[:, i * P:(i + 1) * P], on[:, i, :], e, T1.free, sig=(i == 1))
            o_free[0] = [tk]
            yield 0.7
            a = act(oah[:, hd, :], T1.t[:, 0:T], ACT.Copy, tk)
            d = tt(oal[:, hd, :], T1.t[:, 0:T], oah[:, hd, :].bitcast(F32), S_, a)
            T1.free, T1.held = [a, d], False
            hg_mem["done"] = [d]
            left[pair] -= 1
            grp_done[pair % 2] = [DV.now(), PE.now()]
            vg_done[g % 2] = [DV.now(), PE.now()]

        def group(g):
            steps = 2.4 if g == 0 else 2.0
            finish_pair(2 * (g - 2) + 1)
            pr, t = stream(uh, ul, ready, steps)
            for i in range(2):
                pr[i].free = [act(vb[g % 2][:, i, :], pr[i].t[:, :], ACT.Copy, t, vg_done[g % 2])]
            t_vb = AC.now()
            pr, t = stream(uh, ul, ready, steps)
            for i in range(2):
                gv = gb[g % 2][:, i, :]
                a = act(gv, pr[i].t[:, :], ACT.Sigmoid, t, vg_done[g % 2])
                d = tt(gv, pr[i].t[:, :], gv, M_, a)
                pr[i].free = [d]
                t_gb = tt(gv.rearrange("p (h d) -> p h d", h=4), gv.rearrange("p (h d) -> p h d", h=4),
                          strided(hgn[:, :], [0, 4], [1, 128]), M_, d, t_hgn)
            for b in range(2):
                p = 2 * g + b
                slot = 2 * (p % 2)
                finish_pair(p - 2)
                pr, t = stream(uh, ul, ready, steps)
                for i in range(2):
                    o = qb[:, slot + i, :]
                    a = act(o, pr[i].t[:, 0:T], ACT.Sigmoid, t, grp_done[p % 2])
                    d = tt(o, pr[i].t[:, 0:T], o, M_, a)
                    pr[i].free = [d]
                pr, t = stream(uh, ul, ready, steps)
                for i in range(2):
                    hh = 4 * g + 2 * b + i
                    f, k = Gb[:, slot + i, :], kb[:, slot + i, :]
                    a = act(f, pr[i].t[:, 0:T], ACT.Sigmoid, t, grp_done[p % 2])
                    a2 = act(k, pr[i].t[:, 0:T], ACT.Sigmoid, scale=-1.0)
                    pr[i].free = [a2]
                    ts(k, k, oml[:, hh:hh + 1], None, M_, None, a2)
                    d = ts(f, f, oml[:, hh:hh + 1], lb[:, hh:hh + 1], M_, A_, a)
                fg = Gb[:, slot:slot + 2, :]
                t_ln = act(fg, fg, ACT.Ln, d)
                if p == 0:
                    hg_setup()
                    steps = 2.0
                PE.wait(t_vb, t_gb)
                tasks.extend(scan_head(g, 2 * b + i, t_ln) for i in range(2))

        sgb_free = [[]]

        def attention_gate(n):
            c = slice(512 * n, 512 * (n + 1))
            pr, t = stream(uh, ul, ready, 1.5)
            for i in range(2):
                pr[i].free = [act(X[:, i, c], pr[i].t[:, :], ACT.Sigmoid, t)]
            a = AC.now()
            pr, t = stream(obh, obl, [ob_t[0]] * 4, 1.5)
            for i in range(2):
                pr[i].free = [tt(X[:, i, c], pr[i].t[:, :], X[:, i, c], M_, t, a)]

        for what, g in ORDER:
            (group if what == "G" else attention_gate)(g)

        pr, t_gate = stream(uh, ul, ready, 2)
        drain()
        fz = fence()
        m_area = Area(Z + 8192, END)
        mix = m_area.get("mix", [2, D])
        sg = m_area.get("sg", [2, 512])
        oah, oal = hg_mem["oah"], hg_mem["oal"]
        oa_ready = [hg_mem["done"]] * 16
        mt = {}
        for n in range(4):
            c = slice(512 * n, 512 * (n + 1))
            if n:
                pr, t_gate = stream(uh, ul, ready)
            for i in range(2):
                pr[i].free = [act(sg[:, i, :], pr[i].t[:, :], ACT.Sigmoid, t_gate, DV.now())]
            a = AC.now()
            pr, t = stream(oah, oal, oa_ready)
            for i in range(2):
                d = tt(mix[:, i, c], pr[i].t[:, :], sg[:, i, :], M_, t, a)
                pr[i].free = [d]
                mt[i, n] = tt(mix[:, i, c], mix[:, i, c], X[:, i, c], A_, d)
        tx = [load(PO, X[:, t, :], x_dram[:, t, :], f"xr{t}", mt[0, 3], mt[1, 3]) for t in range(2)]
        DV.wait(tx)
        rm = to_uT(lambda t, k: mix[:, t, k * P:(k + 1) * P], None, lambda t, k: mt[t, k // 4], t_gate)
        ready = [rm[k] for k in range(16)]

        def residual(xh, xl, rdy, steps=1):
            ss = [[], []]
            for n in range(4):
                c = slice(512 * n, 512 * (n + 1))
                pr, t = stream(xh, xl, rdy, steps)
                for i in range(2):
                    d = tt(X[:, i, c], pr[i].t[:, :], X[:, i, c], A_, t)
                    pr[i].free = [d]
                    ss[i].append(stats(i, n, X[:, i, c], d))
            return ss

        ss = residual(uh, ul, ready)

        fence()
        area = Area(Z, END)
        xs = at("xs_b", [2, D], Z)
        rm = normed(xs, ss, lambda k: cst1[:, 16 + k:17 + k], PE.now())
        ready = [rm[k] for k in range(16)]
        fence()
        gh = area.get("gh", [44, T], F32R)
        gl = area.get("gl", [44, T], F32R)
        ya = [area.get(f"ya{i}", [2, T]) for i in range(2)]
        yb = [area.get(f"yb{i}", [2, T]) for i in range(2)]

        def conv3(pr, t, y, j0, y_free):
            for i in range(2):
                j = j0 + i
                p = pr[i].t
                a = act(y[:, i, :], p[:, 0:T], ACT.Identity, t, y_free, scale=cw[:, 2, j:j + 1], bias=cw[:, 3, j:j + 1])
                d = stt(y[:, i, 1:T], p[:, 0:T - 1], cw[:, 1, j:j + 1], y[:, i, 1:T], M_, A_, a)
                d = stt(y[:, i, 2:T], p[:, 0:T - 2], cw[:, 0, j:j + 1], y[:, i, 2:T], M_, A_, d)
                pr[i].free = [d]
            return DV.now()

        ya_free, yb_free = [[], []], [[], []]
        g_ready = []
        for j in range(22):
            a_, b_ = ya[j % 2], yb[j % 2]
            pr, t = stream(uh, ul, ready)
            d = conv3(pr, t, a_, 2 * j, ya_free[j % 2])
            a = act(a_[:, :, :], a_[:, :, :], ACT.Gelu_apprx_tanh, d)
            pr, t = stream(uh, ul, ready)
            d = conv3(pr, t, b_, 44 + 2 * j, yb_free[j % 2])
            d = tt(a_[:, :, :], a_[:, :, :], b_[:, :, :], M_, d, a)
            yb_free[j % 2] = [d]
            o = slice(2 * j, 2 * j + 2)
            a = act(gh[:, o, :], a_[:, :, :], ACT.Copy, d)
            d = tt(gl[:, o, :], a_[:, :, :], gh[:, o, :].bitcast(F32), S_, a)
            ya_free[j % 2] = [a, d]
            g_ready += [d, d]
        ss = residual(gh, gl, g_ready)
        fz = fence()

        area = Area(Z, END)
        xs = area.get("xs_c", [2, D])
        area.o = Z
        lt = [area.get(f"lt{i}", [4, T]) for i in range(4)]
        uN = area.get("uN", [2, 1024])
        vN = area.get("vN", [2, 1024])
        lng = area.get("lng", [1024])
        lnb = area.get("lnb", [1024])
        xc = area.get("xc", [8, T])
        ggr = area.get("ggr", [8, T])
        ho = area.get("ho", [8, T])
        lw = area.get("lw", [32, P])
        wsn = area.get("wsn", [8, P])
        wsT = area.get("wsT", [8, P])
        g1 = at("g1", [D], Z + 16384)
        t_g1 = load(AC, g1[:, :], io["norm_f_g"].partition_broadcast(P), "c_nf", fz)
        t_lw1 = load(PO, lw[:, 0:16, :], io["lru_w_a_2"][0].rearrange("d h c e -> c (d h) e"), "c_lwa", fz)
        t_lw2 = load(PO, lw[:, 16:32, :], io["lru_w_x_2"][0].rearrange("d h c e -> c (d h) e"), "c_lwx", fz)
        t_ws = load(PO, wsn[:, :, :], io["gmlp_w_s_2"][0].rearrange("h p q -> p h q"), "c_ws", fz)
        t_lng = load(PO, lng[:, :], io["gmlp_ln_g_2"][0].partition_broadcast(P), "c_lng", fz)
        t_lnb = load(PO, lnb[:, :], io["gmlp_ln_b_2"][0].partition_broadcast(P), "c_lnb", fz)
        r = [rms(t, ss[t]) for t in range(2)]
        ss = [[], []]
        for t in range(2):
            for j in range(4):
                c = slice(512 * j, 512 * (j + 1))
                d = stt(X[:, t, c], X[:, t, c], rstd[:, t:t + 1], g1[:, c], M_, M_, r[t], t_g1)
                ss[t].append(stats(t, j, X[:, t, c], d))
        rm = normed(xs, ss, lambda k: cst2[:, k:k + 1], PE.now())
        ready = [rm[k] for k in range(16)]
        fence()
        for h in range(0, 8, 4):
            bk = (M0, M1)[h // 4]
            for j in range(4):
                tk = tr(bk.t[:, j * P:(j + 1) * P], wsn[:, h + j, :], t_ws, bk.free, sig=(j == 3))
            e = act(wsT[:, h:h + 4, :], bk.t[:, :].rearrange("p (h q) -> p h q", h=4), ACT.Copy, tk)
            bk.free = [e]
        t_wsT = AC.now()

        for b in range(4):
            pr, t = stream(uh, ul, ready)
            for i in range(2):
                h = 2 * b + i
                p, y = pr[i].t, xc[:, h, :]
                wk = [cst2[:, 32 + 8 * k + h:33 + 8 * k + h] for k in range(4)]
                a = act(y, p[:, 0:T], ACT.Identity, t, scale=wk[2], bias=cst2[:, 64 + h:65 + h])
                d = stt(y[:, 1:T], p[:, 0:T - 1], wk[1], y[:, 1:T], M_, A_, a)
                d = stt(y[:, 2:T], p[:, 0:T - 2], wk[0], y[:, 2:T], M_, A_, d)
                d = stt(y[:, 0:T - 1], p[:, 1:T], wk[3], y[:, 0:T - 1], M_, A_, d)
                pr[i].free = [d]
        t_xc = DV.now()

        def lru(dr, hb):
            R, I, Aa, Th = lt
            yield from hold(M0)
            for q in range(4):
                h = hb + q
                wi = 8 * dr + h
                mm(M0.t[:, 0:T], lw[:, wi, :], xc[:, h, :], True, True, t_xc, t_lw1, t_lw2, M0.free)
                tk = mm(M0.t[:, T:2 * T], lw[:, 16 + wi, :], xc[:, h, :], True, True, sig=True)
                yield 0.5
                a = act(R[:, q, :], M0.t[:, 0:T], ACT.Sigmoid, tk, lru_free[0], bias=cst2[:, 80 + wi:81 + wi])
                b = act(I[:, q, :], M0.t[:, T:2 * T], ACT.Sigmoid, bias=cst2[:, 96 + wi:97 + wi])
                M0.free = [b]
            M0.held = False
            yield 2.0
            for q in range(4):
                wi = 8 * dr + hb + q
                e1 = act(Aa[:, q, :], R[:, q, :], ACT.Exp, AC.now(), scale=nsp[:, wi:wi + 1])
                e2 = act(Th[:, q, :], R[:, q, :], ACT.Tanh, scale=psp[:, wi:wi + 1])
            yield 1.0
            d = tt(R[:, :, :], Aa[:, :, :], Aa[:, :, :], M_, e1, e2)
            d = DV.do(lambda e: e.scalar_tensor_tensor(R[:, :, :], R[:, :, :], 1.0, Th[:, :, :], A_, M_), d)
            i1 = tt(I[:, :, :], I[:, :, :], xc[:, hb:hb + 4, :], M_, b)
            yield 2.0
            a = act(R[:, :, :], R[:, :, :], ACT.Sqrt, d)
            yield 2.0
            d = tt(R[:, :, :], R[:, :, :], I[:, :, :], M_, a, i1)
            for q in range(4):
                h = hb + q
                o = ho[:, h, :] if dr == 0 else Th[:, q, :]
                av, uv = Aa[:, q, :], R[:, q, :]
                if dr:
                    o, av, uv = o[:, ::-1], av[:, ::-1], uv[:, ::-1]
                f = DV.do(lambda e, o=o, av=av, uv=uv: e.tensor_tensor_scan(o, av, uv, 0.0, M_, A_), d)
            if dr:
                f = tt(ho[:, hb:hb + 4, :], ho[:, hb:hb + 4, :], Th[:, :, :], A_, f)
            lru_free[0] = [f]

        lru_free = [[]]
        tasks += [lru(dr, hb) for hb in (0, 4) for dr in (0, 1)]
        pace["active"] = 1
        vs = [[], []]
        for b in range(2):
            pr, t = stream(uh, ul, ready, 1.0)
            for i in range(2):
                v = vN[:, i, 512 * b:512 * (b + 1)]
                a = act(v, pr[i].t[:, :], ACT.Gelu_apprx_tanh, t)
                pr[i].free = [a]
                vs[i].append(stats(i, b, v, a))
        t_vn = []
        for i in range(2):
            a = finish_stats(i, 2, vs[i])
            s = act(sq[:, i:i + 1], mv[:, i, 1:2], ACT.Sqrt, a, bias=eps[:, 0:1])
            d = DV.do(lambda e, i=i: e.reciprocal(rstd[:, i:i + 1], sq[:, i:i + 1]), s)
            d = ts(vN[:, i, :], vN[:, i, :], mv[:, i, 0:1], rstd[:, i:i + 1], S_, M_, d)
            d = tt(vN[:, i, :], vN[:, i, :], lng[:, :], M_, d, t_lng)
            t_vn.append(tt(vN[:, i, :], vN[:, i, :], lnb[:, :], A_, d, t_lnb))
        for b in range(2):
            pr, t_u = stream(uh, ul, ready, 1.0)
            for i in range(2):
                pr[i].free = [act(uN[:, i, 512 * b:512 * (b + 1)], pr[i].t[:, :], ACT.Gelu_apprx_tanh, t_u)]
        t_un = AC.now()
        gm = {}

        def spatial():
            for i in range(2):
                for h0 in (0, 4):
                    for q in range(4):
                        h = h0 + q
                        tk = mm(T1.t[:, q * P:(q + 1) * P], wsT[:, h, :], vN[:, i, h * P:(h + 1) * P], True, True,
                                t_wsT, t_vn[i], T1.free, sig=(q == 3))
                    yield 0.8
                    for q in range(4):
                        h = h0 + q
                        uu = uN[:, i, h * P:(h + 1) * P]
                        gm[i, h] = stt(uu, T1.t[:, q * P:(q + 1) * P], cst2[:, 72 + h:73 + h], uu, A_, M_, tk, t_un)
                    T1.free = [gm[i, h0 + 3]]

        tasks.append(spatial())
        for b in range(4):
            pr, t_u = stream(uh, ul, ready, 1)
            for i in range(2):
                pr[i].free = [act(ggr[:, 2 * b + i, :], pr[i].t[:, 0:T], ACT.Gelu_apprx_tanh, t_u)]
        t_ggr = AC.now()
        drain()
        pace["active"] = 2
        ready = []
        for h0 in (0, 4):
            hs_ = slice(h0, h0 + 4)
            d = tt(ho[:, hs_, :], ho[:, hs_, :], ggr[:, hs_, :], M_, t_ggr, lru_free[0])
            a = act(uh[:, hs_, :], ho[:, hs_, :], ACT.Copy, d, t_u)
            d = tt(ul[:, hs_, :], ho[:, hs_, :], uh[:, hs_, :].bitcast(F32), S_, a, t_u)
            ready += [d] * 4
        rm = to_uT(lambda t, k: uN[:, t, (k - 8) * P:(k - 7) * P], None, lambda t, k: gm[t, k - 8], t_u, ks=range(8, 16, 2))
        ready += [rm[k] for k in range(8, 16)]
        ss = residual(uh, ul, ready)

        fz = fence()
        area = Area(Z, END)
        xn = area.get("xn", [2, D])
        sc = area.get("sc", [2, 16, P])
        g2 = area.get("g2", [D])
        cand = area.get("cand", [16, 16])
        oneh = area.get("oneh", [16, 16])
        tsv = area.get("tsv", [2, 16])
        tif = area.get("tif", [2, 16])
        tiu = area.get("tiu", [2, 16], U32)
        bs = area.get("bs", [16])
        pos = area.get("pos", [16], U32)
        pi = area.get("pi", [16], U32)
        pf = area.get("pf", [16])
        sel = [area.get(f"sel{i}", [16]) for i in range(2)]
        sg8 = area.get("sg8", [1])
        ids = [area.get(f"ids{i}", [128], U32) for i in range(2)]
        gw = [area.get(f"gw{i}", [8, 16]) for i in range(2)]
        dots = [area.get(f"dots{i}", [128]) for i in range(2)]
        qTt = area.get("qTt", [4, T])
        kyT = area.get("kyT", [16, P])
        Ub = [area.get(f"Ub{i}", [D]) for i in range(NU)]
        fu = fz
        kyN = at("kyN", [16, P], Z + 16384)
        t_g2 = load(AC, g2[:, :], io["ffn_norm_g_2"][0].partition_broadcast(P), "c_g2", fz)
        t_ky = load(PO, kyN[:, :, :], io["peer_sub_keys_2"][0].rearrange("h j n k -> n (h j) k"), "c_ky", fz)
        r = [rms(t, ss[t]) for t in range(2)]
        xo = {}
        for j in range(4):
            for t in range(2):
                c = slice(512 * j, 512 * (j + 1))
                xo[t, j] = stt(xn[:, t, c], X[:, t, c], rstd[:, t:t + 1], g2[:, c], M_, M_, r[t], t_g2)
        rm = to_uT(lambda t, k: xn[:, t, k * P:(k + 1) * P], None, lambda t, k: xo[t, k // 4], PE.now())
        ready = [rm[k] for k in range(16)]
        t_xn = DV.now()
        t_g2b = load(AC, g2[:, :], io["final_norm_g_2"].partition_broadcast(P), "c_fin", t_xn)
        for h in range(0, 16, 4):
            bk = (M0, M1)[(h // 4) % 2]
            for j in range(4):
                tk = tr(bk.t[:, j * P:(j + 1) * P], kyN[:, h + j, :], t_ky, bk.free, sig=(j == 3))
            e = act(kyT[:, h:h + 4, :], bk.t[:, :].rearrange("p (h q) -> p h q", h=4), ACT.Copy, tk)
            bk.free = [e]
        t_kyT = AC.now()
        LOWEST = -3.0e38

        def top16(vals, top, idx, *after):
            a = DV.do(lambda e: e.max(top[:, 0:8], vals), *after)
            b = DV.do(lambda e: e.max_index(idx[:, 0:8], top[:, 0:8], vals), a)
            c = DV.do(lambda e: e.match_replace(vals, top[:, 0:8], vals, LOWEST), a, b)
            d = DV.do(lambda e: e.max(top[:, 8:16], vals), c)
            return DV.do(lambda e: e.max_index(idx[:, 8:16], top[:, 8:16], vals), d)

        ids_t, gw_t, sc_t = {}, {}, {}

        def choose(t, h):
            d = DV.now()
            for j in range(2):
                d = top16(sc[:, t, 2 * h + j, :], tsv[:, j, :], tiu[:, j, :], sc_t[h], d)
            d = cp(tif[:, :, :], tiu[:, :, :], d)
            d = tt(cand[:, :, :], strided(tsv[:, 0, :], [1, 16], [0, 16]), strided(tsv[:, 1, :], [0, 16], [1, 16]), A_, d)
            yield 2.2
            d = top16(cand[:, :, :].rearrange("p a b -> p (a b)"), bs[:, :], pos[:, :], d)
            yield 2.2
            for side in range(2):
                op, by = ((ALU.logical_shift_right, 4), (ALU.bitwise_and, 15))[side]
                d = DV.do(lambda e, op=op, by=by: e.tensor_scalar(pi[:, :], pos[:, :], by, None, op), d)
                d = cp(pf[:, :], pi[:, :], d)
                d = tt(oneh[:, :, :], strided(pf[:, :], [1, 16], [0, 16]), strided(iota[:, :], [0, 16], [1, 16]), ALU.is_equal, d, t_io)
                d = tt(oneh[:, :, :], oneh[:, :, :], strided(tif[:, side, :], [0, 16], [1, 16]), M_, d)
                d = DV.do(lambda e, side=side: e.tensor_reduce(sel[side][:, :], oneh[:, :, :], AX, A_), d)
            d = stt(sel[0][:, :], sel[0][:, :], 128.0, sel[1][:, :], M_, A_, d)
            ids_t[t, h] = d = cp(ids[t][:, 16 * h:16 * h + 16], sel[0][:, :], d)
            yield 2.2
            gwv = gw[t][:, h, :]
            d = tt(gwv, bs[:, :], strided(bs[:, 0:1], [0, 16]), S_, d)
            a = act(gwv, gwv, ACT.Exp, d, accum_out=sg8[:, 0:1])
            d = DV.do(lambda e: e.reciprocal(sg8[:, :], sg8[:, :]), a)
            gw_t[t, h] = ts(gwv, gwv, sg8[:, 0:1], None, M_, None, d)

        v_area = Area(u0, Z)
        Vb = [v_area.get(f"Vb{i}", [D]) for i in range(NV)]
        u_sem = [Counter(sem(f"us{i}")) for i in range(NU)]
        v_sem = [Counter(sem(f"vs{i}")) for i in range(NV)]
        eu, ev = io["peer_u_2"][0], io["peer_v_2"][0]
        u_in, v_in, dot_t, act_t, dg_t, v_use, summed = {}, {}, {}, {}, {}, {}, {}
        out_banks = [(M0, M1, T0, T1), (W0, W1, W2, W3)]
        out_sem = Counter(sem("outs"))
        out_d = out[0].rearrange("(t p) d -> p t d", p=P)

        def gather(buf, table, t, k, counter, *after):
            idx = ids[t][:, k:k + 1]
            return PO.dma(lambda e: e.indirect_dma_start(buf[:, :], None, table, bass.IndirectOffsetOnAxis(idx, 0)),
                          counter, *after)

        def get_u(n):
            t, k = divmod(n, 128)
            u_in[n] = gather(Ub[n % NU], eu, t, k, u_sem[n % NU], ids_t[t, k // 16], fu, dot_t.get(n - NU))

        def get_v(n):
            t, k = divmod(n, 128)
            v_in[n] = gather(Vb[n % NV], ev, t, k, v_sem[n % NV], ids_t[t, k // 16], fz, v_use.get(n - NV))

        def dot(n):
            t, k = divmod(n, 128)
            b = Ub[n % NU]
            dot_t[n] = DV.do(lambda e: e.tensor_tensor_reduce(b[:, :], b[:, :], xn[:, t, :], 1.0, 0.0, M_, A_, dots[t][:, k:k + 1]),
                             u_in[n], t_xn)
            if k % GROUP == GROUP - 1:
                h, c = k // 16, slice(k + 1 - GROUP, k + 1)
                a = act(dots[t][:, c], dots[t][:, c], ACT.Gelu_apprx_tanh, dot_t[n])
                act_t[t, k // GROUP] = tt(dots[t][:, c], dots[t][:, c], gw[t][:, h, (k + 1 - GROUP) % 16:k % 16 + 1], M_, a, gw_t[t, h])

        begun, begins = [0], []

        def begin(count, upto):
            for _ in range(count):
                n = begun[0]
                if n >= upto:
                    return
                begun[0] += 1
                if n == 0:
                    for m in range(NU):
                        get_u(m)
                dot(n)
                if n + NU < upto:
                    get_u(n + NU)
                yield 2.3

        pace["active"] = 1
        q_free = [[], []]
        for h in range(8):
            pr, t = stream(uh, ul, ready, 1.7)
            for i in range(2):
                pr[i].free = [act(qTt[:, 2 * (h % 2) + i, :], pr[i].t[:, 0:T], ACT.Copy, t, q_free[h % 2])]
            bk = (M0, M1)[h % 2]
            for t in range(2):
                for j in range(2):
                    hp = 2 * h + j
                    tk = mm(bk.t[:, (2 * t + j) * P:(2 * t + j + 1) * P], qTt[:, 2 * (h % 2) + j, t * P:(t + 1) * P], kyT[:, hp, :],
                            True, True, AC.now(), t_kyT, bk.free, sig=(t == 1 and j == 1))
            sc_t[h] = act(sc[:, :, 2 * h:2 * h + 2, :], bk.t[:, :].rearrange("p (t h q) -> p t h q", t=2, h=2), ACT.Copy, tk)
            bk.free = [sc_t[h]]
            q_free[h % 2] = [tk]
            tasks.append(choose(0, h))
            if h:
                begins.append(begin(6, 16 * h))
                tasks.append(begins[-1])
        tasks[:] = [g for g in tasks if g not in begins]
        fz = fence()

        def accumulate(n):
            t, k = divmod(n, 128)
            dg_t[n] = act(diag[:, n % 4, :], ident[:, :], ACT.Copy, act_t[t, k // GROUP], v_use.get(n - 4), scale=dots[t][:, k:k + 1])
            for j in range(4):
                bk = out_banks[t][j]
                tk = mm(bk.t[:, :], diag[:, n % 4, :], Vb[n % NV][:, 512 * j:512 * (j + 1)], k == 0, k == 127,
                        dg_t[n], v_in[n], bk.free if k == 0 else None, sig=(j == 3 or k == 127))
                summed[t, j] = tk
            v_use[n] = tk

        def finish(t):
            sx = []
            for j in range(4):
                c = slice(512 * j, 512 * (j + 1))
                d = tt(X[:, t, c], out_banks[t][j].t[:, :], X[:, t, c], A_, summed[t, j])
                sx.append(stats(t, j, X[:, t, c], d))
            r = rms(t, sx)
            for j in range(4):
                c = slice(512 * j, 512 * (j + 1))
                d = stt(X[:, t, c], X[:, t, c], rstd[:, t:t + 1], g2[:, c], M_, M_, r, t_g2b)
            SP.dma(lambda e: e.dma_start(out_d[:, t, :], X[:, t, :]), out_sem, d)

        tasks += [choose(1, h) for h in range(8)]
        for n in range(256 + VLAG):
            if n >= VLAG:
                accumulate(n - VLAG)
            while n < 256 and (n // 128, n % 128 // 16) not in gw_t:
                step()
            if n < 256 and n not in u_in:
                get_u(n)
            m = n - VLAG + VAHEAD
            if 0 <= m < 256:
                get_v(m)
            if n < 256 and n not in dot_t:
                dot(n)
            if begun[0] <= n < 126:
                step()
            if n == 127 + VLAG + 4:
                finish(0)
        finish(1)
        SP.wait((out_sem.sem, out_sem.n))

        blk = ctx.enter_context(nc.Block())
        blk.sync(SP.run)
        blk.tensor(PE.run)
        blk.scalar(AC.run)
        blk.vector(DV.run)
        blk.gpsimd(PO.run)


_INS = ['x', 'norm1_g', 'w_in', 'hg_lb_param', 'hg_norm_g', 'w_proj_a', 'w_proj_b', 'w_out', 'norm2_g', 'w_up',
        'conv_w', 'conv_b', 'w_down', 'norm_f_g', 'mix_norm_g_2', 'w_in_2', 'conv_w_2', 'conv_b_2', 'lru_w_a_2',
        'lru_b_a_2', 'lru_w_x_2', 'lru_b_x_2', 'lru_lambda_2', 'gmlp_ln_g_2', 'gmlp_ln_b_2', 'gmlp_w_s_2',
        'gmlp_b_s_2', 'w_out_2', 'ffn_norm_g_2', 'peer_w_q_2', 'peer_sub_keys_2', 'peer_u_2', 'peer_v_2',
        'final_norm_g_2']


def kernel(**inputs):
    import concourse.bacc as _bacc
    from concourse.bass_utils import run_bass_kernel_spmd as _run

    nc = _bacc.Bacc("TRN2", target_bir_lowering=False, num_devices=1)
    arrays, args = {}, {}
    for name in _INS:
        a = np.ascontiguousarray(inputs[name])
        arrays[f"in_{name}"] = a
        args[name] = nc.dram_tensor(f"in_{name}", a.shape, mybir.dt.from_np(a.dtype), kind="ExternalInput").ap()
    arrays["in_consts"] = shape_constants()
    args["consts"] = nc.dram_tensor("in_consts", (P, CONST_W), F32, kind="ExternalInput").ap()
    out = nc.dram_tensor("out_0", (1, T, D), F32, kind="ExternalOutput").ap()
    program(nc, args, out)
    r = _run(nc, [arrays], core_ids=[0])
    return r.results[0]["out_0"]
```
